# Optimizing a Trainium2 kernel written in Bass

```python
import jax, jax.numpy as jnp
from jax import lax
import numpy as np
import math

D_MODEL = 1024
BATCH = 1
SEQ = 256
DEPTH = 1

PLE_DIM = 256
MLA_HEADS = 8
MLA_NOPE_DIM = 64
MLA_ROPE_DIM = 32
MLA_V_DIM = 64
Q_LORA_RANK = 384
KV_LORA_RANK = 256
SB_HEADS = 8
SB_HEAD_DIM = 64
MLA_WIDTH = MLA_HEADS * MLA_V_DIM
SB_WIDTH = SB_HEADS * SB_HEAD_DIM
MIX_WIDTH = MLA_WIDTH + SB_WIDTH
IN_SPLITS = (Q_LORA_RANK,
             Q_LORA_RANK + KV_LORA_RANK,
             Q_LORA_RANK + KV_LORA_RANK + MLA_ROPE_DIM,
             Q_LORA_RANK + KV_LORA_RANK + MLA_ROPE_DIM + SB_WIDTH,
             Q_LORA_RANK + KV_LORA_RANK + MLA_ROPE_DIM + 2 * SB_WIDTH)
IN_COLS = Q_LORA_RANK + KV_LORA_RANK + MLA_ROPE_DIM + 3 * SB_WIDTH
ROPE_THETA = 10000.0
Q_BLOCK = 128
N_EXPERTS = 32
TOP_K = 4
D_FF = 1024
SWIGLU_LIMIT = 7.0
SWIGLU_ALPHA = 1.702
EXPERT_BLOCK = 128
RMS_EPS = 1e-6
MAX_POS_OFFSET = 4096


def rmsnorm(x, g):
    xf = x.astype(jnp.float32)
    y = xf * lax.rsqrt(jnp.mean(xf * xf, axis=-1, keepdims=True) + RMS_EPS)
    return (y * g.astype(jnp.float32)).astype(x.dtype)

def rope_tables(positions):
    inv_freq = ROPE_THETA ** (-jnp.arange(0, MLA_ROPE_DIM, 2, dtype=jnp.float32) / MLA_ROPE_DIM)
    ang = positions.astype(jnp.float32)[..., None] * inv_freq
    return jnp.cos(ang), jnp.sin(ang)

def apply_rope(x, cos, sin):
    xf = x.astype(jnp.float32)
    x1, x2 = jnp.split(xf, 2, axis=-1)
    return jnp.concatenate([x1 * cos - x2 * sin, x2 * cos + x1 * sin], axis=-1).astype(x.dtype)

def to_blocks(a):
    b, h, s, d = a.shape
    return jnp.moveaxis(a.reshape(b, h, s // Q_BLOCK, Q_BLOCK, d), 2, 0)

def from_blocks(o):
    n, b, h, qb, d = o.shape
    return jnp.moveaxis(o, 0, 2).reshape(b, h, n * qb, d).transpose(0, 2, 1, 3).reshape(b, n * qb, h * d)

def mixer_heads(q_nope, q_rope, k_nope, k_rope, v_mla, q_sb, k_sb, v_sb):
    seq = k_nope.shape[2]
    n_blk = seq // Q_BLOCK
    key_pos = jnp.arange(seq)
    mla_scale = (MLA_NOPE_DIM + MLA_ROPE_DIM) ** -0.5
    sb_scale = SB_HEAD_DIM ** -0.5

    def block(args):
        bi, qn, qr, qs = args
        q_pos = bi * Q_BLOCK + jnp.arange(Q_BLOCK)
        s = (jnp.einsum('bhqd,bhkd->bhqk', qn, k_nope, preferred_element_type=jnp.float32)
             + jnp.einsum('bhqr,bkr->bhqk', qr, k_rope, preferred_element_type=jnp.float32)) * mla_scale
        causal = key_pos[None, :] <= q_pos[:, None]
        w = jax.nn.softmax(jnp.where(causal, s, -jnp.inf), axis=-1)
        o_m = jnp.einsum('bhqk,bhkd->bhqd', w.astype(v_mla.dtype), v_mla)
        z = jnp.einsum('bhqd,bhkd->bhqk', qs, k_sb, preferred_element_type=jnp.float32) * sb_scale
        strict = key_pos[None, :] < q_pos[:, None]
        log_not = jnp.where(strict, jax.nn.log_sigmoid(-z), 0.0)
        after = lax.cumsum(log_not, axis=3, reverse=True) - log_not
        log_a = jnp.where(strict, jax.nn.log_sigmoid(z) + after, -jnp.inf)
        o_s = jnp.einsum('bhqk,bhkd->bhqd', jnp.exp(log_a).astype(v_sb.dtype), v_sb)
        return o_m, o_s

    o_m, o_s = lax.map(block, (jnp.arange(n_blk), to_blocks(q_nope), to_blocks(q_rope), to_blocks(q_sb)))
    return from_blocks(o_m), from_blocks(o_s)

def moe(u, w_router, b_router, w_gu, b_gu, w_dn, b_dn):
    b, s, d = u.shape
    t = b * s
    xt = u.reshape(t, d)
    logits = jnp.dot(xt, w_router, preferred_element_type=jnp.float32) + b_router.astype(jnp.float32)
    top_logit, top_e = lax.top_k(logits, TOP_K)
    gate = jax.nn.softmax(top_logit, axis=-1)
    n_pairs = t * TOP_K
    flat_e = top_e.reshape(-1)
    flat_tok = jnp.arange(n_pairs, dtype=jnp.int32) // TOP_K
    flat_g = gate.reshape(-1)
    order = jnp.argsort(flat_e)
    sorted_e = flat_e[order]
    counts = jnp.bincount(flat_e, length=N_EXPERTS)
    padded = (counts + EXPERT_BLOCK - 1) // EXPERT_BLOCK * EXPERT_BLOCK
    pad_end = jnp.cumsum(padded)
    pad_start = pad_end - padded
    start = jnp.cumsum(counts) - counts
    dest = pad_start[sorted_e] + jnp.arange(n_pairs) - start[sorted_e]
    n_blocks = -(-n_pairs // EXPERT_BLOCK) + N_EXPERTS
    n_rows = n_blocks * EXPERT_BLOCK
    row_tok = jnp.full((n_rows,), t, jnp.int32).at[dest].set(flat_tok[order])
    row_gate = jnp.zeros((n_rows,), jnp.float32).at[dest].set(flat_g[order])
    block_e = jnp.minimum(jnp.searchsorted(pad_end, jnp.arange(n_blocks) * EXPERT_BLOCK, side='right'),
                          N_EXPERTS - 1)
    x_pad = jnp.concatenate([xt, jnp.zeros((1, d), xt.dtype)], axis=0)
    xb = x_pad[row_tok].reshape(n_blocks, EXPERT_BLOCK, d)

    def expert_block(args):
        e, xs = args
        hh = jnp.dot(xs, w_gu[e]) + b_gu[e]
        glu, lin = jnp.split(hh, 2, axis=-1)
        glu = jnp.minimum(glu, SWIGLU_LIMIT)
        lin = jnp.clip(lin, -SWIGLU_LIMIT, SWIGLU_LIMIT)
        act = glu * jax.nn.sigmoid(SWIGLU_ALPHA * glu) * (lin + 1.0)
        return jnp.dot(act, w_dn[e]) + b_dn[e]

    yb = lax.map(expert_block, (block_e, xb))
    yr = yb.reshape(n_rows, d) * row_gate[:, None].astype(yb.dtype)
    y = jax.ops.segment_sum(yr, row_tok, num_segments=t + 1)[:t]
    return y.reshape(b, s, d)

def first_inputs(seed: int = 0) -> dict:
    key = jax.random.key(seed)
    ks = jax.random.split(key, 24)

    def nrm(k, shape, scale):
        return jax.random.normal(k, shape, jnp.float32) * scale

    def gain(k, shape):
        return 1.0 + 0.05 * jax.random.normal(k, shape, jnp.float32)

    offsets = jax.random.randint(ks[2], (BATCH, 1), 0, MAX_POS_OFFSET, dtype=jnp.int32)
    positions = offsets + jnp.arange(SEQ, dtype=jnp.int32)[None, :]
    return {
        'x': nrm(ks[0], (BATCH, SEQ, D_MODEL), 1.0),
        'p': nrm(ks[1], (DEPTH, BATCH, SEQ, PLE_DIM), 1.0),
        'positions': positions,
        'w_in': nrm(ks[3], (DEPTH, D_MODEL, IN_COLS), D_MODEL ** -0.5),
        'g_attn': gain(ks[4], (DEPTH, D_MODEL)),
        'g_cq': gain(ks[5], (DEPTH, Q_LORA_RANK)),
        'w_uq': nrm(ks[6], (DEPTH, Q_LORA_RANK, MLA_HEADS * (MLA_NOPE_DIM + MLA_ROPE_DIM)), Q_LORA_RANK ** -0.5),
        'g_ckv': gain(ks[7], (DEPTH, KV_LORA_RANK)),
        'w_ukv': nrm(ks[8], (DEPTH, KV_LORA_RANK, MLA_HEADS * (MLA_NOPE_DIM + MLA_V_DIM)), KV_LORA_RANK ** -0.5),
        'g_out_mla': gain(ks[9], (DEPTH, MLA_WIDTH)),
        'g_out_sb': gain(ks[10], (DEPTH, SB_WIDTH)),
        'w_o': nrm(ks[11], (DEPTH, MIX_WIDTH, D_MODEL), MIX_WIDTH ** -0.5),
        'g_moe': gain(ks[12], (DEPTH, D_MODEL)),
        'w_router': nrm(ks[13], (DEPTH, D_MODEL, N_EXPERTS), D_MODEL ** -0.5),
        'b_router': nrm(ks[14], (DEPTH, N_EXPERTS), 0.01),
        'w_gu': nrm(ks[15], (DEPTH, N_EXPERTS, D_MODEL, 2 * D_FF), D_MODEL ** -0.5),
        'b_gu': nrm(ks[16], (DEPTH, N_EXPERTS, 2 * D_FF), 0.01),
        'w_dn': nrm(ks[17], (DEPTH, N_EXPERTS, D_FF, D_MODEL), D_FF ** -0.5),
        'b_dn': nrm(ks[18], (DEPTH, N_EXPERTS, D_MODEL), 0.01),
        'g_ple': gain(ks[19], (DEPTH, D_MODEL)),
        'w_ple_gate': nrm(ks[20], (DEPTH, D_MODEL, D_MODEL), D_MODEL ** -0.5),
        'w_ple_proj': nrm(ks[21], (DEPTH, PLE_DIM, D_MODEL), PLE_DIM ** -0.5),
        'g_final': gain(ks[22], (D_MODEL,)),
    }

def first_block(x, p, positions, w_in, g_attn, g_cq, w_uq, g_ckv, w_ukv, g_out_mla, g_out_sb, w_o,
              g_moe, w_router, b_router, w_gu, b_gu, w_dn, b_dn, g_ple, w_ple_gate, w_ple_proj, g_final):
    b, s, _ = x.shape
    cos, sin = rope_tables(positions)

    def heads_first(a):
        return jnp.swapaxes(a, 1, 2)

    h = x
    for i in range(DEPTH):
        u = rmsnorm(h, g_attn[i])
        c_q, c_kv, k_r, q_s, k_s, v_s = jnp.split(u @ w_in[i], IN_SPLITS, axis=-1)
        q = (rmsnorm(c_q, g_cq[i]) @ w_uq[i]).reshape(b, s, MLA_HEADS, MLA_NOPE_DIM + MLA_ROPE_DIM)
        kv = (rmsnorm(c_kv, g_ckv[i]) @ w_ukv[i]).reshape(b, s, MLA_HEADS, MLA_NOPE_DIM + MLA_V_DIM)
        q_nope = q[..., :MLA_NOPE_DIM]
        q_rope = apply_rope(q[..., MLA_NOPE_DIM:], cos[:, :, None, :], sin[:, :, None, :])
        k_nope = kv[..., :MLA_NOPE_DIM]
        v_m = kv[..., MLA_NOPE_DIM:]
        k_rope = apply_rope(k_r, cos, sin)
        sb_shape = (b, s, SB_HEADS, SB_HEAD_DIM)
        o_m, o_s = mixer_heads(heads_first(q_nope), heads_first(q_rope), heads_first(k_nope), k_rope,
                               heads_first(v_m), heads_first(q_s.reshape(sb_shape)),
                               heads_first(k_s.reshape(sb_shape)), heads_first(v_s.reshape(sb_shape)))
        mixed = jnp.concatenate([rmsnorm(o_m, g_out_mla[i]), rmsnorm(o_s, g_out_sb[i])], axis=-1)
        h = h + mixed @ w_o[i]
        h = h + moe(rmsnorm(h, g_moe[i]), w_router[i], b_router[i], w_gu[i], b_gu[i], w_dn[i], b_dn[i])
        u = rmsnorm(h, g_ple[i])
        h = h + jax.nn.sigmoid(u @ w_ple_gate[i]) * (p[i] @ w_ple_proj[i])
    return rmsnorm(h, g_final)


N_ATTN_HEADS = 8
HEAD_DIM = 64
D_ATTN = N_ATTN_HEADS * HEAD_DIM
MOBA_BLOCK = 256
MOBA_TOPK = 3
Q_CHUNK = 16
N_BUCKETS = 32
MAX_EXACT = N_BUCKETS // 2
MAX_DISTANCE = 128
D_LRU = D_MODEL // 2
N_LRU_BLOCKS = 8
LRU_BLOCK = D_LRU // N_LRU_BLOCKS
LRU_CONV_W = 4
LRU_C = 8.0
D_MIX = D_ATTN + D_LRU
D_IN_PROJ = 3 * D_ATTN + 2 * D_LRU
D_FF_2 = 2816
FFN_CONV_W = 3


def rms_norm(x, g):
    xf = x.astype(jnp.float32)
    y = xf * lax.rsqrt(jnp.mean(xf * xf, axis=-1, keepdims=True) + RMS_EPS)
    return (y * g.astype(jnp.float32)).astype(x.dtype)

def causal_dwconv(x, w, b):
    width, ch = w.shape
    y = lax.conv_general_dilated(
        x, w[:, None, :].astype(x.dtype), window_strides=(1,), padding=[(width - 1, 0)],
        dimension_numbers=("NWC", "WIO", "NWC"), feature_group_count=ch)
    return y + b.astype(x.dtype)

def t5_bucket(dist):
    n = jnp.maximum(dist, 0)
    nf = jnp.maximum(n, 1).astype(jnp.float32)
    large = MAX_EXACT + (jnp.log(nf / MAX_EXACT) / math.log(MAX_DISTANCE / MAX_EXACT)
                         * (N_BUCKETS - MAX_EXACT)).astype(jnp.int32)
    large = jnp.minimum(large, N_BUCKETS - 1)
    return jnp.where(n < MAX_EXACT, n, large)

def moba_attention(q, k, v, rel_bias):
    B, H, S, dh = q.shape
    nb = -(-S // MOBA_BLOCK)
    pad = nb * MOBA_BLOCK - S
    k_pad = jnp.pad(k, ((0, 0), (0, 0), (0, pad), (0, 0)))
    v_pad = jnp.pad(v, ((0, 0), (0, 0), (0, pad), (0, 0)))
    k_blocks = k_pad.reshape(B, H, nb, MOBA_BLOCK, dh)
    v_blocks = v_pad.reshape(B, H, nb, MOBA_BLOCK, dh)
    k_mean = jnp.mean(k_blocks.astype(jnp.float32), axis=3)
    top = min(MOBA_TOPK, nb)
    scale = HEAD_DIM ** -0.5
    key_off = jnp.arange(MOBA_BLOCK, dtype=jnp.int32)
    b_i = jnp.arange(B)[:, None, None, None]
    h_i = jnp.arange(H)[None, :, None, None]
    bias_T = rel_bias.astype(jnp.float32).T

    def chunk(c):
        q0 = c * Q_CHUNK
        qc = lax.dynamic_slice_in_dim(q, q0, Q_CHUNK, axis=2)
        q_pos = q0 + jnp.arange(Q_CHUNK, dtype=jnp.int32)
        own = q0 // MOBA_BLOCK
        gate = jnp.einsum("bhqd,bhnd->bhqn", qc.astype(jnp.float32), k_mean)
        past = jnp.arange(nb) < own
        gate = jnp.where(past[None, None, None, :], gate, -jnp.inf)
        _, idx = lax.top_k(gate, top)
        valid = idx < own
        k_sel = k_blocks[b_i, h_i, idx]
        v_sel = v_blocks[b_i, h_i, idx]
        s_sel = jnp.einsum("bhqd,bhqjkd->bhqjk", qc, k_sel,
                           preferred_element_type=jnp.float32) * scale
        k_pos_sel = idx[..., None] * MOBA_BLOCK + key_off
        bucket_sel = t5_bucket(q_pos[None, None, :, None, None] - k_pos_sel)
        s_sel = s_sel + bias_T[h_i[..., None], bucket_sel]
        s_sel = jnp.where(valid[..., None], s_sel, -jnp.inf)
        k_own = lax.dynamic_slice_in_dim(k_pad, own * MOBA_BLOCK, MOBA_BLOCK, axis=2)
        v_own = lax.dynamic_slice_in_dim(v_pad, own * MOBA_BLOCK, MOBA_BLOCK, axis=2)
        s_own = jnp.einsum("bhqd,bhkd->bhqk", qc, k_own,
                           preferred_element_type=jnp.float32) * scale
        dist_own = q_pos[:, None] - (own * MOBA_BLOCK + key_off)[None, :]
        s_own = s_own + jnp.transpose(rel_bias.astype(jnp.float32)[t5_bucket(dist_own)], (2, 0, 1))[None]
        s_own = jnp.where((dist_own >= 0)[None, None], s_own, -jnp.inf)
        logits = jnp.concatenate([s_sel.reshape(B, H, Q_CHUNK, top * MOBA_BLOCK), s_own], axis=-1)
        p = jax.nn.softmax(logits, axis=-1).astype(v.dtype)
        p_sel = p[..., :top * MOBA_BLOCK].reshape(B, H, Q_CHUNK, top, MOBA_BLOCK)
        p_own = p[..., top * MOBA_BLOCK:]
        return (jnp.einsum("bhqjk,bhqjkd->bhqd", p_sel, v_sel)
                + jnp.einsum("bhqk,bhkd->bhqd", p_own, v_own))

    outs = lax.map(chunk, jnp.arange(S // Q_CHUNK))
    return jnp.transpose(outs, (1, 2, 0, 3, 4)).reshape(B, H, S, dh)

def rg_lru(x, w_r, b_r, w_i, b_i, lam):
    B, S, _ = x.shape
    xf = x.astype(jnp.float32)
    xb = xf.reshape(B, S, N_LRU_BLOCKS, LRU_BLOCK)
    r = jax.nn.sigmoid(jnp.einsum("bsnc,ncd->bsnd", xb, w_r.astype(jnp.float32)).reshape(B, S, D_LRU)
                       + b_r.astype(jnp.float32))
    i = jax.nn.sigmoid(jnp.einsum("bsnc,ncd->bsnd", xb, w_i.astype(jnp.float32)).reshape(B, S, D_LRU)
                       + b_i.astype(jnp.float32))
    log_a = -LRU_C * r * jax.nn.softplus(-lam.astype(jnp.float32))
    a = jnp.exp(log_a)
    u = jnp.sqrt(-jnp.expm1(2.0 * log_a)) * (i * xf)

    def combine(left, right):
        a1, b1 = left
        a2, b2 = right
        return a1 * a2, a2 * b1 + b2

    _, h = lax.associative_scan(combine, (a, u), axis=1)
    return h.astype(x.dtype)

def second_inputs(seed: int = 0) -> dict:
    key = jax.random.key(seed)
    ks = jax.random.split(key, 24)
    nrm = lambda k, shape, s: jax.random.normal(k, shape, jnp.float32) * s
    u_a = jax.random.uniform(ks[10], (DEPTH, D_LRU), jnp.float32, 0.9, 0.999)
    base = u_a ** (1.0 / LRU_C)
    lam = jnp.log(base) - jnp.log1p(-base)
    return {
        "x": nrm(ks[0], (BATCH, SEQ, D_MODEL), 1.0),
        "g_pre_mix": 1.0 + nrm(ks[1], (DEPTH, D_MODEL), 0.05),
        "w_in": nrm(ks[2], (DEPTH, D_MODEL, D_IN_PROJ), D_MODEL ** -0.5),
        "rel_bias": nrm(ks[3], (N_BUCKETS, N_ATTN_HEADS), 0.3),
        "w_conv_lru": nrm(ks[4], (DEPTH, LRU_CONV_W, D_LRU), LRU_CONV_W ** -0.5),
        "b_conv_lru": nrm(ks[5], (DEPTH, D_LRU), 0.02),
        "w_r": nrm(ks[6], (DEPTH, N_LRU_BLOCKS, LRU_BLOCK, LRU_BLOCK), LRU_BLOCK ** -0.5),
        "b_r": nrm(ks[7], (DEPTH, D_LRU), 0.02),
        "w_i": nrm(ks[8], (DEPTH, N_LRU_BLOCKS, LRU_BLOCK, LRU_BLOCK), LRU_BLOCK ** -0.5),
        "b_i": nrm(ks[9], (DEPTH, D_LRU), 0.02),
        "lam": lam,
        "w_out": nrm(ks[11], (DEPTH, D_MIX, D_MODEL), D_MIX ** -0.5),
        "g_post_mix": 1.0 + nrm(ks[12], (DEPTH, D_MODEL), 0.05),
        "g_pre_ffn": 1.0 + nrm(ks[13], (DEPTH, D_MODEL), 0.05),
        "w_up": nrm(ks[14], (DEPTH, D_MODEL, 2 * D_FF_2), D_MODEL ** -0.5),
        "w_conv_ffn": nrm(ks[15], (DEPTH, FFN_CONV_W, 2 * D_FF_2), FFN_CONV_W ** -0.5),
        "b_conv_ffn": nrm(ks[16], (DEPTH, 2 * D_FF_2), 0.02),
        "w_down": nrm(ks[17], (DEPTH, D_FF_2, D_MODEL), D_FF_2 ** -0.5),
        "g_post_ffn": 1.0 + nrm(ks[18], (DEPTH, D_MODEL), 0.05),
    }

def second_block(x, g_pre_mix, w_in, rel_bias, w_conv_lru, b_conv_lru, w_r, b_r, w_i, b_i, lam,
              w_out, g_post_mix, g_pre_ffn, w_up, w_conv_ffn, b_conv_ffn, w_down, g_post_ffn):
    B, S, _ = x.shape
    for l in range(DEPTH):
        h = rms_norm(x, g_pre_mix[l])
        proj = h @ w_in[l].astype(h.dtype)
        q, k, v, xr, gr = jnp.split(
            proj, [D_ATTN, 2 * D_ATTN, 3 * D_ATTN, 3 * D_ATTN + D_LRU], axis=-1)
        to_heads = lambda t: jnp.transpose(t.reshape(B, S, N_ATTN_HEADS, HEAD_DIM), (0, 2, 1, 3))
        attn = moba_attention(to_heads(q), to_heads(k), to_heads(v), rel_bias)
        attn = jnp.transpose(attn, (0, 2, 1, 3)).reshape(B, S, D_ATTN)
        xr = causal_dwconv(xr, w_conv_lru[l], b_conv_lru[l])
        lru = rg_lru(xr, w_r[l], b_r[l], w_i[l], b_i[l], lam[l]) * jax.nn.gelu(gr, approximate=True)
        mix = jnp.concatenate([attn, lru], axis=-1) @ w_out[l].astype(h.dtype)
        x = x + rms_norm(mix, g_post_mix[l])
        h = rms_norm(x, g_pre_ffn[l])
        up = causal_dwconv(h @ w_up[l].astype(h.dtype), w_conv_ffn[l], b_conv_ffn[l])
        c_u, c_g = jnp.split(up, 2, axis=-1)
        ffn = (jax.nn.gelu(c_g, approximate=True) * c_u) @ w_down[l].astype(h.dtype)
        x = x + rms_norm(ffn, g_post_ffn[l])
    return x


def setup_inputs(seed=0):
    out = dict(first_inputs(seed))
    for name, value in second_inputs(seed + 1).items():
        if name != "x":
            out[name + "_2"] = value
    return out


def reference(
    x, p, positions, w_in, g_attn, g_cq, w_uq, g_ckv, w_ukv, g_out_mla, g_out_sb, w_o, g_moe,
    w_router, b_router, w_gu, b_gu, w_dn, b_dn, g_ple, w_ple_gate, w_ple_proj, g_final,
    g_pre_mix_2, w_in_2, rel_bias_2, w_conv_lru_2, b_conv_lru_2, w_r_2, b_r_2, w_i_2, b_i_2,
    lam_2, w_out_2, g_post_mix_2, g_pre_ffn_2, w_up_2, w_conv_ffn_2, b_conv_ffn_2, w_down_2,
    g_post_ffn_2,
):
    x = first_block(
        x, p, positions, w_in, g_attn, g_cq, w_uq, g_ckv, w_ukv, g_out_mla, g_out_sb, w_o,
        g_moe, w_router, b_router, w_gu, b_gu, w_dn, b_dn, g_ple, w_ple_gate, w_ple_proj,
        g_final,
    )
    return second_block(
        x, g_pre_mix_2, w_in_2, rel_bias_2, w_conv_lru_2, b_conv_lru_2, w_r_2, b_r_2, w_i_2,
        b_i_2, lam_2, w_out_2, g_post_mix_2, g_pre_ffn_2, w_up_2, w_conv_ffn_2, b_conv_ffn_2,
        w_down_2, g_post_ffn_2,
    )


_drawn_inputs = setup_inputs


def setup_inputs(seed=0):
    import zlib

    import numpy as np

    out = dict(_drawn_inputs(seed))
    spreads = {}
    factors = {'b_gu': 8.0,
     'b_dn': 8.0,
     'g_ple': 6.768,
     'b_r_2': 23.438,
     'b_i_2': 8.0,
     'b_conv_ffn_2': 3.468}
    for name, (base, spread) in spreads.items():
        noise = np.random.default_rng([zlib.crc32(name.encode()), seed]).standard_normal(out[name].shape)
        drawn = base * np.exp(spread * noise) if base else spread * noise
        out[name] = __import__('jax').numpy.asarray(drawn.astype(out[name].dtype))
    for name, factor in factors.items():
        out[name] = (out[name] * factor).astype(out[name].dtype)
    return out
```

```python
import math
from contextlib import ExitStack

import numpy as np

import concourse.bass as bass
from concourse import mybir

F32 = mybir.dt.float32
I32 = mybir.dt.int32
U32 = mybir.dt.uint32
ALU = mybir.AluOpType
ACT = mybir.ActivationFunctionType
AX = mybir.AxisListType

P = 128
T = 256
D = 1024
KD = D // P
NE = 32
CAP = 64
NSLOT = 12
SLOTW = 2048
NEG = -1.0e30
EPS = 1e-6
TWO_PI = 2.0 * math.pi
C1 = 6.28125
C2 = float(np.float32(np.floor((TWO_PI - C1) * 2.0 ** 21) / 2.0 ** 21))
C3 = TWO_PI - C1 - C2
MAGIC = 12582912.0


class Queue:

    def __init__(self, sem):
        self.sem, self.items, self.n = sem, [], 0

    def __call__(self, fn, *waits, sig=True):
        self.items.append((flat(waits), fn, sig))
        self.n += sig
        return (self.sem, self.n) if sig else None

    def last(self):
        return (self.sem, self.n)

    def emit(self, eng):
        seen = {}
        for waits, fn, sig in self.items:
            for sem, v in waits:
                if seen.get(sem, 0) < v:
                    eng.wait_ge(sem, v)
                    seen[sem] = v
            ins = fn(eng)
            if sig is True:
                ins.then_inc(self.sem, 1)

    def raw(self, fn, *waits):
        self.items.append((flat(waits), fn, False))


class Round:

    def __init__(self, sem):
        self.sem, self.items, self.n = sem, [], 0

    def __call__(self, fn, *waits, sig=1):
        self.items.append((flat(waits), fn, sig))
        self.n += sig
        return (self, self.n)

    def emit(self, eng, i):
        seen = {}
        for waits, fn, sig in self.items:
            for q, v in waits:
                if seen.get(q, 0) < v:
                    eng.wait_ge(q.sem, i * q.n + v)
                    seen[q] = v
            ins = fn(eng, i)
            if sig:
                ins.then_inc(self.sem, sig)


def flat(waits):
    out = []
    for w in waits:
        if w is None:
            continue
        if isinstance(w, list):
            out += flat(w)
        else:
            out.append(w)
    return out


def bucket_table():
    oh = np.zeros((33, 512), np.float32)
    for m in range(512):
        n = 255 - m
        if n < 0:
            oh[32, m] = 1.0
            continue
        b = n if n < 16 else min(31, 16 + int(math.log(n / 16.0) / math.log(128 / 16) * 16 + 1e-9))
        oh[b, m] = 1.0
    return oh


def inv_freq_table():
    f = 10000.0 ** (-np.arange(0, 32, 2, dtype=np.float64) / 32)
    return f.astype(np.float32).reshape(1, 16)


def build_program(nc, I, out, stop=None):
    ctx = ExitStack()
    with ctx:
        def sb(name, shape, dt=F32):
            return ctx.enter_context(nc.sbuf_tensor(name, shape, dt))

        def sem(name):
            return ctx.enter_context(nc.semaphore(name))

        def bc(ap, shape):
            return ap.broadcast_to(shape)

        ring = sb("ring", [P, NSLOT, SLOTW])
        h = sb("h", [P, 2, D])
        u = sb("u", [P, 2, D])
        uT = sb("uT", [P, KD, T])
        arena = sb("arena", [P, 20480])
        ident = sb("ident", [P, P])
        cols = sb("cols", [P, 264])
        msk = sb("msk", [P, 3, T])
        sm = sb("sm", [P, 320])
        wr = sb("wr", [P, KD, NE])
        ps = ctx.enter_context(nc.psum_tensor("ps", [P, 8, 512], F32))
        skew = nc.dram_tensor("skew", [8, P, 512], F32, kind="Internal").ap()

        PE = Queue(sem("s_pe"))
        A = Queue(sem("s_act"))
        V = Queue(sem("s_dve"))
        G = Queue(sem("s_pool"))
        SP = Queue(sem("s_sp"))
        slot_sem = [sem(f"s_slot{i}") for i in range(NSLOT)]

        def ar(off, *shape):
            n = int(np.prod(shape))
            v = arena[:, off:off + n]
            if len(shape) == 2:
                v = v.rearrange("p (a b) -> p a b", a=shape[0])
            elif len(shape) == 3:
                v = v.rearrange("p (a b c) -> p a b c", a=shape[0], b=shape[1])
            return v

        def dma(q, name, dst, src, *waits):
            s = sem(name)
            q(lambda e: e.dma_start(dst, src).then_inc(s, 16), *waits, sig=False)
            return (s, 16)

        loads, freed = [], {}

        def load(src, cols_n, **shape):
            n = len(loads)
            dst = ring[:, n % NSLOT, 0:cols_n]
            if shape:
                dst = dst.rearrange("p (a b) -> p a b", **shape)
            loads.append((dst, src))
            return n

        def slot(n, a=None):
            v = ring[:, n % NSLOT, :]
            return v if a is None else v[:, 0:a[0] * a[1]].rearrange("p (a b) -> p a b", a=a[0])

        def landed(n):
            return (slot_sem[n % NSLOT], 16 * (n // NSLOT + 1))

        def mm(o, l, r, start, stop, *waits, sig=False):
            return PE(lambda e: e.matmul(o, l, r, start=start, stop=stop), *waits, sig=sig)

        def tr(o, i, *waits, sig=False):
            n = i.shape[0]
            return PE(lambda e: e.transpose(o, i, ident[0:n, 0:n]), t_ident, *waits, sig=sig)

        def act(o, i, f, *waits, **kw):
            return A(lambda e: e.activation(o, i, f, **kw), *waits)

        def vcopy(o, i, *waits):
            return V(lambda e: e.tensor_copy(o, i), *waits)

        def vts(o, i, s1, s2, op0, op1, *waits):
            if op1 is None:
                return V(lambda e: e.tensor_scalar(o, i, s1, None, op0), *waits)
            return V(lambda e: e.tensor_scalar(o, i, s1, s2, op0, op1), *waits)

        def vtt(o, a, b, op, *waits):
            return V(lambda e: e.tensor_tensor(o, a, b, op), *waits)

        def vstt(o, a, s, b, op0, op1, *waits):
            return V(lambda e: e.scalar_tensor_tensor(out=o, in0=a, scalar=s, in1=b, op0=op0, op1=op1), *waits)

        def vred(o, i, op, *waits):
            return V(lambda e: e.tensor_reduce(o, i, AX.X, op), *waits)

        def vrecip(o, i, *waits):
            return V(lambda e: e.reciprocal(o, i), *waits)

        bank_free = [None] * 8
        state = {"bank": 0}

        def nb():
            b = state["bank"]
            state["bank"] = (b + 1) % 8
            return b

        t_x = dma(SP, "d_x", h[:, :, :], I["x"][0].rearrange("(t p) d -> p t d", p=P))
        stage = ar(0, 3, P)
        rows = {}
        small = []
        pos_row = [0, 0]

        def rowload(name, src, n):
            tile, r = pos_row
            if r + n > P:
                tile, r = tile + 1, 0
            rows[name] = (tile, r)
            small.append(dma(G, f"d_{name}", stage[r:r + n, tile, :], src))
            pos_row[0], pos_row[1] = tile, r + n

        def vec(name, k):
            return I[name].rearrange("a (k p) -> (a k) p", p=P)

        t_z = V(lambda e: e.memset(stage[:, :, :], 0.0))
        for name, k in (("g_attn", 8), ("g_cq", 3), ("g_ckv", 2), ("g_out_mla", 4), ("g_out_sb", 4), ("g_moe", 8),
                        ("g_ple", 8), ("g_pre_mix_2", 8), ("b_conv_lru_2", 4), ("b_r_2", 4), ("b_i_2", 4),
                        ("lam_2", 4), ("g_pre_ffn_2", 8)):
            rowload(name, vec(name, k), k)
        rowload("w_conv_lru_2", I["w_conv_lru_2"].rearrange("a j (k p) -> (a j k) p", p=P), 16)
        pos_row[0], pos_row[1] = 1, 0
        rowload("w_conv_ffn_2", I["w_conv_ffn_2"][0, 0:2].rearrange("j (k p) -> (j k) p", p=P), 88)
        pos_row[0], pos_row[1] = 2, 0
        rowload("w_conv_ffn_2b", I["w_conv_ffn_2"][0, 2:3].rearrange("j (k p) -> (j k) p", p=P), 44)
        rowload("b_conv_ffn_2", vec("b_conv_ffn_2", 44), 44)
        G.items = [([t_z] + w, f, s) for w, f, s in G.items]
        col0 = (0, 88, 176)

        def col(name, k=0):
            tile, r = rows[name]
            c = col0[tile] + r + k
            return cols[:, c:c + 1]

        posi = sb("posi", [P, 2], I32)
        t_pos = [dma(G, f"d_pos{t}", posi[:, t:t + 1], I["positions"][0, t * P:(t + 1) * P].rearrange("(p a) -> p a", a=1))
                 for t in range(2)]
        invf = sm[:, 0:16]
        t_inv = dma(G, "d_inv", invf, bc(I["c_inv_freq"], [P, 16]))
        brt = sm[:, 16:48]
        t_brt = dma(G, "d_brt", brt, bc(I["b_router"], [P, 32]))
        oht = ar(1024, 512)[0:33, :]
        rel = ar(1536, 16)[0:33, 0:8]
        t_rel0 = V(lambda e: e.memset(ar(1536, 16)[:, :], NEG))
        t_oht = dma(G, "d_oht", oht, I["c_bucket"])
        t_rel = dma(G, "d_rel", rel[0:32, :], I["rel_bias_2"], t_rel0)

        t1 = G(lambda e: e.memset(ident[:, :], 0.0))
        t_ident = G(lambda e: e.affine_select(out=ident[:, :], in_=ident[:, :], compare_op=ALU.not_equal, fill=1.0,
                                              base=0, pattern=[[-1, P]], channel_multiplier=1), t1)
        t1 = G(lambda e: e.memset(msk[:, 0:2, :], 0.0))
        t2 = G(lambda e: e.memset(msk[:, 2, :], -1.0))
        t3 = G(lambda e: e.affine_select(out=msk[:, 0, :], in_=msk[:, 0, :], compare_op=ALU.is_ge, fill=NEG, base=P,
                                         pattern=[[-1, T]], channel_multiplier=1), t1, t2)
        t3 = G(lambda e: e.affine_select(out=msk[:, 1, :], in_=msk[:, 1, :], compare_op=ALU.is_gt, fill=NEG, base=P,
                                         pattern=[[-1, T]], channel_multiplier=1))
        t_msk = G(lambda e: e.affine_select(out=msk[:, 2, :], in_=msk[:, 2, :], compare_op=ALU.is_gt, fill=0.0, base=P,
                                            pattern=[[-1, T]], channel_multiplier=1))
        iota = sm[:, 48:112]
        t_iota = G(lambda e: e.iota(iota, [[1, CAP]], base=0, channel_multiplier=0,
                                    allow_small_or_imprecise_dtypes=True))

        onec = sm[:, 152:153]
        t_one = G(lambda e: e.memset(onec, 1.0))

        for tile in range(3):
            b = nb()
            t = tr(ps[:, b, 0:P], stage[:, tile, :], small, bank_free[b], sig=True)
            bank_free[b] = vcopy(cols[:, col0[tile]:col0[tile] + 88], ps[:, b, 0:88], t)
        t_cols = bank_free[b]

        t_rb = []
        R = ar(2048, 8, 512)
        for hd in range(8):
            b = nb()
            t = mm(ps[:, b, :], bc(rel[:, hd:hd + 1], [33, P]), oht, True, True, t_rel, t_oht, bank_free[b], sig=True)
            bank_free[b] = act(R[:, hd, :], ps[:, b, :], ACT.Copy, t)
            t_rb.append(bank_free[b])
        t_skew = dma(G, "d_skew", skew.rearrange("h p m -> p h m"), R, t_rb)

        t_wr = dma(G, "d_wr", wr[:, :, :], I["w_router"][0].rearrange("(k p) e -> p k e", p=P))

        def kload(src, k0, nk, c0, nc_):
            return load(src[k0 * P:(k0 + nk) * P, c0:c0 + nc_].rearrange("(k p) n -> p k n", p=P), nk * nc_, a=nk)

        w_in, w_o = I["w_in"][0], I["w_o"][0]
        L_a = [(kload(w_in, k, n, 0, 672), k, n) for k, n in ((0, 3), (3, 3), (6, 2))]
        L_uq = [(kload(I["w_uq"][0], 0, 2, 0, 768), 0, 2), (kload(I["w_uq"][0], 2, 1, 0, 768), 2, 1)]
        L_ukv = kload(I["w_ukv"][0], 0, 2, 0, 1024)
        L_qk = [kload(w_in, 2 * j, 2, 672, 1024) for j in range(4)]
        L_v = [kload(w_in, 4 * j, 4, 1696, 512) for j in range(2)]
        L_o = [kload(w_o, 2 * j, 2, 0, 1024) for j in range(4)]
        L_gu, L_dn = {}, {}

        def load_gu(e):
            L_gu[e] = [load(I["w_gu"][0, e, k * P:(k + 1) * P, :], 2048) for k in range(KD)]

        def load_dn(e):
            L_dn[e] = [kload(I["w_dn"][0, e], 2 * j, 2, 0, 1024) for j in range(4)]

        load_gu(0)
        for e in range(1, NE):
            load_gu(e)
            load_dn(e - 1)
        load_dn(NE - 1)
        L_pg = [kload(I["w_ple_gate"][0], 2 * j, 2, 0, 1024) for j in range(4)]
        L_pp = kload(I["w_ple_proj"][0], 0, 2, 0, 1024)
        w2 = I["w_in_2"][0]
        L2_qk = [kload(w2, 2 * j, 2, 0, 1024) for j in range(4)]
        L2_v = [kload(w2, 4 * j, 4, 1024, 512) for j in range(2)]
        L2_xg = [kload(w2, 2 * j, 2, 1536, 1024) for j in range(4)]
        L2_o = [kload(I["w_out_2"][0], 2 * j, 2, 0, 1024) for j in range(4)]
        wup = I["w_up_2"][0]
        L2_up = []
        for i in range(11):
            for half in range(2):
                c0 = half * 2816 + i * 256
                L2_up.append(load(wup[:, c0:c0 + 256].rearrange("(k p) n -> p k n", p=P), 2048, a=8))
        L2_dn = [kload(I["w_down_2"][0], 2 * j, 2, 0, 1024) for j in range(11)]

        ss = sm[:, 112:116]
        rs = sm[:, 116:120]
        rn = [0]

        def rstd(parts, *waits):
            ts = []
            for c, (src, junk, n) in enumerate(parts):
                ts.append(act(junk, src, ACT.Square, *waits, accum_out=ss[:, c:c + 1]))
            tv = []
            for c, (src, junk, n) in enumerate(parts):
                tv.append(vts(rs[:, c:c + 1], ss[:, c:c + 1], 1.0 / n, EPS, ALU.mult, ALU.add, ts[c]))
            n = len(parts)
            t = act(rs[:, 0:n], rs[:, 0:n], ACT.Sqrt, tv)
            return vrecip(rs[:, 0:n], rs[:, 0:n], t)

        def norm_rows(src, dst, junk, groups, *waits):
            parts = [(src[:, t, a:b], junk[:, t, a:b], b - a) for a, b in groups for t in range(2)]
            t_r = rstd(parts, *waits)
            toks = []
            for c, (a, b, t) in enumerate((a, b, t) for a, b in groups for t in range(2)):
                toks.append(vts(dst[:, t, a:b], src[:, t, a:b], rs[:, c:c + 1], None, ALU.mult, None, t_r))
            return toks

        def to_columns(src, dst, k0, nk, gain, waits, free):
            toks = []
            for k in range(0, nk, 2):
                b = nb()
                m = min(2, nk - k)
                for j in range(m):
                    for t in range(2):
                        last = tr(ps[:, b, j * T + t * P:j * T + (t + 1) * P],
                                  src[:, t, (k0 + k + j) * P:(k0 + k + j + 1) * P],
                                  waits, bank_free[b], sig=(j == m - 1 and t == 1))
                if (k // 2) % 2 == 0:
                    for j in range(m):
                        tk = vts(dst[:, k + j, :], ps[:, b, j * T:(j + 1) * T], gain(k + j), None, ALU.mult, None,
                                 last, t_cols, free)
                else:
                    for j in range(m):
                        tk = act(dst[:, k + j, :], ps[:, b, j * T:(j + 1) * T], ACT.Copy, last, t_cols, free,
                                 scale=gain(k + j))
                bank_free[b] = tk
                toks.append(tk)
            return toks

        def rows_product(xT, nk, slots, per, ncols, waits):
            width = min(512, ncols)
            nn = -(-ncols // width)
            bs = [[nb() for _ in range(nn)] for _ in range(2)]
            last = None
            for k in range(nk):
                s = slots[k // per]
                w = slot(s, (per, ncols))
                for t in range(2):
                    for n in range(nn):
                        b = bs[t][n]
                        c1 = min((n + 1) * width, ncols)
                        end = k == nk - 1
                        free = k % per == per - 1 and t == 1 and n == nn - 1
                        tok = mm(ps[:, b, 0:c1 - n * width], xT[:, k, t * P:(t + 1) * P], w[:, k % per, n * width:c1],
                                 k == 0, end, waits, landed(s), bank_free[b] if k == 0 else None, sig=end or free)
                        if free or (end and t == 1 and n == nn - 1):
                            freed[s] = tok
                        last = tok or last
            return bs, last

        def columns_product(xT, slots, per, ncols, m, bank_ap, waits, sig):
            for k in range(KD):
                w = slot(slots[k // per], (per, ncols))
                tok = mm(bank_ap, w[:, k % per, m * P:(m + 1) * P], xT[:, k, :], k == 0, k == KD - 1,
                         waits, landed(slots[k // per]), sig=(k == KD - 1))
            return tok

        t_u = norm_rows(h, u, u, [(0, D)], t_x)
        t_uT = to_columns(u, uT, 0, KD, lambda k: col("g_attn", k), t_u, None)

        qrow = ar(0, 2, 768)
        krow = ar(1536, 2, 768)
        qT = ar(3072, 8, T)
        kT = ar(5120, 8, T)
        vm = ar(7168, 2, 512)
        qsT = ar(8192, 4, T)
        ksT = ar(9216, 4, T)
        vs = ar(10240, 2, 512)
        SM = ar(11264, 3072)
        Z = ar(14336, 3072)
        L = ar(17408, 3072)
        prow = SM[:, 0:1344].rearrange("p (t n) -> p t n", t=2)
        rp = SM[:, 1344:1344 + 2 * 8 * 16 * 2].rearrange("p (a t h d) -> p a t h d", a=2, t=2, h=8)
        rk = SM[:, 2432:2432 + 128].rearrange("p (a t d) -> p a t d", a=4, t=2)
        cT = Z[:, 0:1280].rearrange("p (k t) -> p k t", k=5)
        cs = L[:, 0:64].rearrange("p (a t d) -> p a t d", a=2, t=2)
        ang = L[:, 64:96].rearrange("p (t d) -> p t d", t=2)
        ak = L[:, 96:128].rearrange("p (t d) -> p t d", t=2)
        posf = L[:, 128:130]

        t = vcopy(posf, posi[:, :], t_pos)
        ta = []
        for j in range(2):
            ta.append(vts(ang[:, j, :], invf, posf[:, j:j + 1], None, ALU.mult, None, t, t_inv))
        t = vts(ak, ang, 1.0 / TWO_PI, None, ALU.mult, None, ta)
        t = vts(ak, ak, MAGIC, None, ALU.add, None, t)
        t = vts(ak, ak, -MAGIC, None, ALU.add, None, t)
        for c in (C1, C2, C3):
            t = vstt(ang, ak, -c, ang, ALU.mult, ALU.add, t)
        t = vts(ang, ang, 3.1415925, -3.1415925, ALU.min, ALU.max, t)
        t_sin = act(cs[:, 1], ang, ACT.Sin, t)
        t = vts(ak, ang, -1.0, None, ALU.mult, None, t)
        t = vtt(ak, ak, ang, ALU.max, t)
        t = vts(ak, ak, -1.0, math.pi / 2, ALU.mult, ALU.add, t)
        t_cos = act(cs[:, 0], ak, ACT.Sin, t)
        t_cs = [t_sin, t_cos]

        bs = [[nb(), nb()] for _ in range(2)]
        for s, k0, n in L_a:
            w = slot(s, (n, 672))
            for k in range(k0, k0 + n):
                for t in range(2):
                    for c, (a, b_) in enumerate(((0, 384), (384, 672))):
                        last = mm(ps[:, bs[t][c], 0:b_ - a], uT[:, k, t * P:(t + 1) * P], w[:, k - k0, a:b_],
                                  k == 0, k == KD - 1, t_uT, landed(s), bank_free[bs[t][c]] if k == 0 else None,
                                  sig=(t == 1 and c == 1))
            freed[s] = last
        t_pr = []
        for t in range(2):
            bank_free[bs[t][0]] = act(prow[:, t, 0:384], ps[:, bs[t][0], 0:384], ACT.Copy, last)
            bank_free[bs[t][1]] = vcopy(prow[:, t, 384:672], ps[:, bs[t][1], 0:288], last)
            t_pr += [bank_free[bs[t][0]], bank_free[bs[t][1]]]

        for half, dst in ((0, qsT), (1, ksT)):
            for j in range(0, 4, 2):
                b = nb()
                for m in range(2):
                    tk = columns_product(uT, L_qk, 2, 1024, half * 4 + j + m, ps[:, b, m * T:(m + 1) * T],
                                         [t_uT, bank_free[b]], True)
                bank_free[b] = act(dst[:, j:j + 2, :], ps[:, b, :].rearrange("p (a b) -> p a b", a=2), ACT.Copy, tk)
            t_qsk = bank_free[b]
        for s in L_qk:
            freed[s] = tk
        bs, last = rows_product(uT, KD, L_v, 4, 512, t_uT)
        t_vs = []
        for t in range(2):
            bank_free[bs[t][0]] = act(vs[:, t, :], ps[:, bs[t][0], :], ACT.Copy, last)
            t_vs.append(bank_free[bs[t][0]])

        t_c = norm_rows(prow, prow, ar(17408 + 256, 2, 640), [(0, 384), (384, 640)], t_pr)
        t_cT = to_columns(prow, cT, 0, 5, lambda k: col("g_cq", k) if k < 3 else col("g_ckv", k - 3), t_c, None)

        def rope(x1, x2, o1, o2, c, s, tmp1, tmp2, *waits):
            a = vtt(tmp1, x2, s, ALU.mult, *waits)
            b_ = vtt(tmp2, x1, s, ALU.mult, *waits)
            c1 = vtt(o1, x1, c, ALU.mult, a, b_)
            c2 = vtt(o2, x2, c, ALU.mult, a, b_)
            d1 = vtt(o1, o1, tmp1, ALU.subtract, c1)
            d2 = vtt(o2, o2, tmp2, ALU.add, c2)
            return [d1, d2]

        t_kr = rope(prow[:, :, 640:656], prow[:, :, 656:672], prow[:, :, 640:656], prow[:, :, 656:672],
                    cs[:, 0], cs[:, 1], rk[:, 0], rk[:, 1], t_pr, t_cs)

        bs = [[nb(), nb()] for _ in range(2)]
        for s, k0, n in L_uq:
            w = slot(s, (n, 768))
            for k in range(k0, k0 + n):
                for t in range(2):
                    for c in range(2):
                        last = mm(ps[:, bs[t][c], 0:384], cT[:, k, t * P:(t + 1) * P], w[:, k - k0, c * 384:(c + 1) * 384],
                                  k == 0, k == 2, t_cT, landed(s), bank_free[bs[t][c]] if k == 0 else None,
                                  sig=(t == 1 and c == 1))
            freed[s] = last
        t_q = []
        for t in range(2):
            for c in range(2):
                b = bs[t][c]
                bank_free[b] = act(qrow[:, t, c * 384:(c + 1) * 384], ps[:, b, 0:384], ACT.Copy, last, t_skew, t_cols)
                t_q.append(bank_free[b])
        bs = [[nb(), nb()] for _ in range(2)]
        w = slot(L_ukv, (2, 1024))
        for k in range(2):
            for t in range(2):
                for c in range(2):
                    last = mm(ps[:, bs[t][c], :], cT[:, 3 + k, t * P:(t + 1) * P], w[:, k, c * 512:(c + 1) * 512],
                              k == 0, k == 1, t_cT, landed(L_ukv), bank_free[bs[t][c]] if k == 0 else None,
                              sig=(t == 1 and c == 1))
        freed[L_ukv] = last
        kh = krow.rearrange("p t (h d) -> p t h d", h=8)
        qh = qrow.rearrange("p t (h d) -> p t h d", h=8)
        vh = vm.rearrange("p t (h d) -> p t h d", h=8)
        t_k = []
        for t in range(2):
            for c in range(2):
                b = bs[t][c]
                src = ps[:, b, :].rearrange("p (h d) -> p h d", h=4)
                t_k.append(vcopy(kh[:, t, 4 * c:4 * c + 4, 0:64], src[:, :, 0:64], last, t_skew, t_cols))
                bank_free[b] = vcopy(vh[:, t, 4 * c:4 * c + 4, :], src[:, :, 64:128], last)
                t_k.append(bank_free[b])
            t_k.append(vcopy(kh[:, t, :, 64:96], bc(prow[:, t, 640:672].unsqueeze(1), [P, 8, 32]), t_kr))
        t_qr = []
        for t in range(2):
            cb = bc(cs[:, 0, t].unsqueeze(1), [P, 8, 16])
            sb_ = bc(cs[:, 1, t].unsqueeze(1), [P, 8, 16])
            t_qr += rope(qh[:, t, :, 64:80], qh[:, t, :, 80:96], qh[:, t, :, 64:80], qh[:, t, :, 80:96],
                         cb, sb_, rp[:, 0, t], rp[:, 1, t], t_q, t_cs)

        def heads_to_columns(src, dst, waits):
            toks = []
            for hd in range(0, 8, 2):
                b = nb()
                for j in range(2):
                    for t in range(2):
                        last = tr(ps[0:96, b, j * T + t * P:j * T + (t + 1) * P],
                                  src[:, t, (hd + j) * 96:(hd + j + 1) * 96], waits, bank_free[b],
                                  sig=(j == 1 and t == 1))
                o, i = dst[0:96, hd:hd + 2, :], ps[0:96, b, :].rearrange("p (a b) -> p a b", a=2)
                bank_free[b] = act(o, i, ACT.Copy, last, t_cols, t_skew) if hd % 4 else vcopy(o, i, last, t_cols, t_skew)
                toks.append(bank_free[b])
            return toks

        t_qT = heads_to_columns(qrow, qT, t_qr)
        t_kT = heads_to_columns(krow, kT, t_k)

        SBS = 64 ** -0.5
        MLS = 96 ** -0.5

        def halves(buf):
            return (buf[:, 0:1024].rearrange("p (h k) -> p h k", h=8),
                    buf[:, 1024:3072].rearrange("p (h k) -> p h k", h=8))

        def pair_scores(qx, kx, waits):
            b0 = [nb(), nb()]
            for i in range(4):
                for par in range(2):
                    pp = slice(64 * par, 64 * par + 64)
                    last = mm(ps[:, b0[par], i * P:(i + 1) * P], qx[pp, i, 0:P], kx[pp, i, 0:P], True, True, waits,
                              bank_free[b0[par]], sig=(i == 3))
            b1 = [[nb(), nb()], [nb(), nb()]]
            for i in range(4):
                for par in range(2):
                    pp = slice(64 * par, 64 * par + 64)
                    b = b1[par][i // 2]
                    last = mm(ps[:, b, (i % 2) * T:(i % 2) * T + T], qx[pp, i, P:T], kx[pp, i, :], True, True, waits,
                              bank_free[b], sig=(i == 3))
            return b0, b1, last

        b0, b1, last = pair_scores(qsT, ksT, [t_qsk])
        Z0, Z1 = halves(Z)
        L0, L1 = halves(L)
        t_zc = []
        for par in range(2):
            bank_free[b0[par]] = act(Z0[:, 4 * par:4 * par + 4, :], ps[:, b0[par], :].rearrange("p (a b) -> p a b", a=4),
                                     ACT.Copy, last, t_q, t_k, scale=SBS)
            t_zc.append(bank_free[b0[par]])
            for i in range(2):
                b = b1[par][i]
                bank_free[b] = act(Z1[:, 4 * par + 2 * i:4 * par + 2 * i + 2, :],
                                   ps[:, b, :].rearrange("p (a b) -> p a b", a=2), ACT.Copy, last, t_q, t_k, scale=SBS)
                t_zc.append(bank_free[b])
        t = act(L, Z, ACT.Abs, t_zc, t_qr, t_kr)
        t = act(L, L, ACT.Exp, t, scale=-1.0)
        t = act(L, L, ACT.Ln, t, bias=1.0)
        t = vstt(L, Z, 0.0, L, ALU.max, ALU.add, t)
        tm = [vtt(L0, L0, bc(msk[:, 2, P:T].unsqueeze(1), [P, 8, P]), ALU.mult, t, t_msk),
              vtt(L1, L1, bc(msk[:, 2, :].unsqueeze(1), [P, 8, T]), ALU.mult, t, t_msk)]
        Q = ar(0, 3072)
        Q0, Q1 = halves(Q)

        bm0 = [nb(), nb()]
        for hd in range(8):
            b = bm0[hd // 4]
            last0 = mm(ps[:, b, (hd % 4) * P:(hd % 4 + 1) * P], qT[0:96, hd, 0:P], kT[0:96, hd, 0:P], True, True,
                       t_qT, t_kT, bank_free[b], sig=(hd % 4 == 3))
        bm1 = [nb() for _ in range(4)]
        for hd in range(8):
            b = bm1[hd // 2]
            last1 = mm(ps[:, b, (hd % 2) * T:(hd % 2 + 1) * T], qT[0:96, hd, P:T], kT[0:96, hd, :], True, True,
                       t_qT, t_kT, bank_free[b], sig=(hd % 2 == 1))
        S0, S1 = halves(SM)
        t_s = []
        for j in range(2):
            bank_free[bm0[j]] = vstt(S0[:, 4 * j:4 * j + 4, :], ps[:, bm0[j], :].rearrange("p (a b) -> p a b", a=4), MLS,
                                     bc(msk[:, 0, P:T].unsqueeze(1), [P, 4, P]), ALU.mult, ALU.add, last0, t_msk, t_qr, t_k, t_cT)
            t_s.append(bank_free[bm0[j]])
        for j in range(4):
            bank_free[bm1[j]] = vstt(S1[:, 2 * j:2 * j + 2, :], ps[:, bm1[j], :].rearrange("p (a b) -> p a b", a=2), MLS,
                                     bc(msk[:, 0, :].unsqueeze(1), [P, 2, T]), ALU.mult, ALU.add, last1, t_msk, t_qr, t_k, t_cT)
            t_s.append(bank_free[bm1[j]])

        mx = sm[:, 120:136]
        rsum = sm[:, 136:152]

        def softmax(buf, waits):
            s0, s1 = halves(buf)
            m = [vred(mx[:, 0:8], s0, ALU.max, waits), vred(mx[:, 8:16], s1, ALU.max, waits)]
            d = [vtt(s0, s0, bc(mx[:, 0:8].unsqueeze(2), [P, 8, P]), ALU.subtract, m),
                 vtt(s1, s1, bc(mx[:, 8:16].unsqueeze(2), [P, 8, T]), ALU.subtract, m)]
            x = act(buf, buf, ACT.Exp, d)
            r = [vred(rsum[:, 0:8], s0, ALU.add, x), vred(rsum[:, 8:16], s1, ALU.add, x)]
            return x, vrecip(rsum, rsum, r)

        t_e, t_r = softmax(SM, t_s)

        t_sc = []
        for lb, qb, n in ((L0, Q0, P), (L1, Q1, T)):
            for hd in range(8):
                o, i = qb[:, hd, ::-1], lb[:, hd, ::-1]
                t_sc.append(V(lambda e, o=o, i=i, n=n: e.tensor_tensor_scan(o, bc(onec, [P, n]), i, 0.0, ALU.mult, ALU.add),
                              tm, t_qT, t_kT, t_one))
        t = vtt(Q, Q, Z, ALU.add, t_sc)
        t = [vtt(Q0, Q0, bc(msk[:, 1, P:T].unsqueeze(1), [P, 8, P]), ALU.add, t),
             vtt(Q1, Q1, bc(msk[:, 1, :].unsqueeze(1), [P, 8, T]), ALU.add, t)]
        t_w = act(Q, Q, ACT.Exp, t)

        def weigh(buf, order, PT, v, waits, ptfree, vwaits):
            s0, s1 = halves(buf)
            blocks = []
            for hd in range(8):
                blocks += [(hd, 0, s0[:, order(hd), :]), (hd, 1, s1[:, order(hd), 0:P]), (hd, 2, s1[:, order(hd), P:T])]
            toks = [None] * 24
            for g in range(0, 24, 4):
                b = nb()
                for j in range(4):
                    last = tr(ps[:, b, j * P:(j + 1) * P], blocks[g + j][2], waits, bank_free[b], sig=(j == 3))
                o = PT[:, g * P:(g + 4) * P]
                bank_free[b] = act(o, ps[:, b, :], ACT.Copy, last, ptfree) if (g // 4) % 2 else vcopy(o, ps[:, b, :], last, ptfree)
                for j in range(4):
                    toks[g + j] = bank_free[b]
            bo = [nb(), nb()]
            pt = PT.rearrange("p (h a q) -> p h a q", h=8, a=3)
            vv = v.rearrange("p t (h d) -> p t h d", h=8)
            for hd in range(8):
                last = mm(ps[:, bo[0], hd * 64:hd * 64 + 64], pt[:, hd, 0, :], vv[:, 0, hd, :], True, True,
                          toks[3 * hd:3 * hd + 3], bank_free[bo[0]], vwaits)
                mm(ps[:, bo[1], hd * 64:hd * 64 + 64], pt[:, hd, 1, :], vv[:, 0, hd, :], True, False, bank_free[bo[1]])
                last = mm(ps[:, bo[1], hd * 64:hd * 64 + 64], pt[:, hd, 2, :], vv[:, 1, hd, :], False, True, sig=(hd == 7))
            return bo, last

        PT = ar(3072, 3072)
        mixed = u
        bo, last = weigh(SM, lambda hd: hd, PT, vm, [t_e], [last0, last1], [t_k])
        t_m = []
        for t in range(2):
            o = mixed[:, t, 0:512].rearrange("p (h d) -> p h d", h=8)
            i = ps[:, bo[t], :].rearrange("p (h d) -> p h d", h=8)
            bank_free[bo[t]] = vtt(o, i, bc(rsum[:, 8 * t:8 * t + 8].unsqueeze(2), [P, 8, 64]), ALU.mult, last, t_r, t_uT)
            t_m.append(bank_free[bo[t]])
        PT2 = ar(11264, 3072)
        bo, last = weigh(Q, lambda hd: 4 * (hd % 2) + hd // 2, PT2, vs, [t_w], [last, PE.last()], t_vs)
        for t in range(2):
            bank_free[bo[t]] = vcopy(mixed[:, t, 512:1024], ps[:, bo[t], :], last, t_uT)
            t_m.append(bank_free[bo[t]])

        t_mn = norm_rows(mixed, mixed, uT[:, :, :].rearrange("p a b -> p (a b)").rearrange("p (t d) -> p t d", t=2),
                         [(0, 512), (512, 1024)], t_m)
        t_mT = to_columns(mixed, uT, 0, KD, lambda k: col("g_out_mla", k) if k < 4 else col("g_out_sb", k - 4), t_mn,
                          [PE.last()])
        bs, last = rows_product(uT, KD, L_o, 2, 1024, t_mT)
        t_h = []
        for t in range(2):
            for n in range(2):
                b = bs[t][n]
                hs = h[:, t, n * 512:(n + 1) * 512]
                bank_free[b] = vtt(hs, hs, ps[:, b, :], ALU.add, last)
                t_h.append(bank_free[b])

        def finish(waits, src=h):
            return dma(SP, "d_out", out[0].rearrange("(t p) d -> p t d", p=P), src[:, :, :], waits)

        def run():
            q = Queue(SP.sem)
            q.items = list(SP.items[:1])
            for n, (dst, src) in enumerate(loads):
                w = []
                if n == L_pg[0] and stop != "attn":
                    q.raw(lambda e: most.__setitem__(q, e.value_load(over, min_val=0, max_val=T - 1)), t_over)
                    rounds(q, OD)
                if n >= NSLOT:
                    if n - NSLOT not in freed:
                        break
                    w = [freed[n - NSLOT]]
                s = slot_sem[n % NSLOT]
                q.items.append((w, lambda e, d=dst, s_=src, sm_=s: e.dma_start(d, s_).then_inc(sm_, 16), False))
            q.items += SP.items[1:]
            SP.items = q.items
            SP.items.append(([done], lambda e: e.wait_ge(*done), False))
            block = ctx.enter_context(nc.Block())

            @block.sync
            def _(e):
                SP.emit(e)

            @block.gpsimd
            def _(e):
                G.emit(e)

            @block.scalar
            def _(e):
                A.emit(e)

            @block.vector
            def _(e):
                V.emit(e)

            @block.tensor
            def _(e):
                PE.emit(e)

        if stop == "attn":
            done = finish(t_h)
            return run()

        posm = sm[:, 160:224].rearrange("p (t e) -> p t e", t=2)
        gate = sm[:, 224:288].rearrange("p (t e) -> p t e", t=2)
        t_u = norm_rows(h, u, u, [(0, D)], t_h, last, t_mT)
        t_uT = to_columns(u, uT, 0, KD, lambda k: col("g_moe", k), t_u, [last])
        S = ar(0, 2, NE, CAP)
        GT = ar(4096, NE, T)
        bgu = ar(12288, 2048)
        xg = [ar(14336 + 2048 * i, KD, 4 * CAP) for i in range(2)]
        glu, lin, sig, actv = (ar(18432 + 512 * i, 512) for i in range(4))
        uTf = uT[:, :, :].rearrange("p k t -> p (k t)")
        actT = [uTf[:, 512 * i:512 * i + 512].rearrange("p (j m) -> p j m", j=4) for i in range(2)]
        yb = [uTf[:, 1024 + 512 * i:1536 + 512 * i] for i in range(2)]
        lg = ar(18432, 2, NE)
        v8 = ar(18496, 2, 8)
        i8 = ar(18512, 2, 8).bitcast(U32)
        f8 = ar(18528, 2, 8)
        e8 = ar(18544, 2, 8)
        z8 = ar(18560, 4)
        oh = ar(18576, 2, NE)
        mk = ar(18640, 2, NE)
        tri = ar(18704, P)
        gT = ar(18840, T)
        bdn = ar(19200, D)
        i32 = ar(20224, NE)
        Sg = arena[:, 14336:18432].rearrange("p (e c s) -> p e c s", e=NE, c=2)

        t_sb = [PE.last(), V.last(), A.last()]
        t0 = G(lambda e: e.memset(tri, 1.0), t_sb)
        t_tri = G(lambda e: e.affine_select(out=tri, in_=tri, compare_op=ALU.is_ge, fill=0.0, base=0,
                                            pattern=[[1, P]], channel_multiplier=-1), t0)
        t_i32 = G(lambda e: e.iota(i32, [[1, NE]], base=0, channel_multiplier=0, allow_small_or_imprecise_dtypes=True))
        t_bz = V(lambda e: e.memset(bgu, 0.0), t_sb)
        t_bgu = dma(G, "d_bgu", bgu[0:NE, :], I["b_gu"][0], t_bz)
        t_bdn = dma(G, "d_bdn", bdn[0:NE, :], I["b_dn"][0])

        t_g = []
        b = nb()
        for t in range(2):
            for k in range(KD):
                last = mm(ps[:, b, t * NE:(t + 1) * NE], uT[:, k, t * P:(t + 1) * P], wr[:, k, :], k == 0, k == KD - 1,
                          t_uT, t_wr, bank_free[b], sig=(k == KD - 1))
        t_lg = bank_free[b] = vtt(lg, ps[:, b, 0:2 * NE].rearrange("p (t e) -> p t e", t=2),
                                  bc(brt.unsqueeze(1), [P, 2, NE]), ALU.add, last, t_brt, t_sb)
        for t in range(2):
            a = V(lambda e, t=t: e.max(v8[:, t, :], lg[:, t, :]), t_lg)
            c = V(lambda e, t=t: e.max_index(i8[:, t, :], v8[:, t, :], lg[:, t, :]), a)
            c = vcopy(f8[:, t, :], i8[:, t, :], c)
            a = vts(z8[:, t:t + 1], v8[:, t, 0:1], -1.0, None, ALU.mult, None, a)
            a = act(e8[:, t, 0:4], v8[:, t, 0:4], ACT.Exp, a, bias=z8[:, t:t + 1], accum_out=z8[:, 2 + t:3 + t])
            a = vrecip(z8[:, 2 + t:3 + t], z8[:, 2 + t:3 + t], a)
            a = vts(e8[:, t, 0:4], e8[:, t, 0:4], z8[:, 2 + t:3 + t], None, ALU.mult, None, a)
            g = vts(gate[:, t, :], i32, f8[:, t, 0:1], e8[:, t, 0:1], ALU.is_equal, ALU.mult, a, c, t_i32)
            for j in range(1, 4):
                o = vts(oh[:, t, :], i32, f8[:, t, j:j + 1], e8[:, t, j:j + 1], ALU.is_equal, ALU.mult, g)
                g = vtt(gate[:, t, :], gate[:, t, :], oh[:, t, :], ALU.add, o)
            t_g.append(g)
        t_mk = vts(mk, gate, 0.0, None, ALU.is_gt, None, t_g)
        b = nb()
        mm(ps[:, b, 0:NE], tri, mk[:, 0, :], True, True, t_mk, t_tri, bank_free[b])
        mm(ps[:, b, NE:2 * NE], bc(onec, [P, P]), mk[:, 0, :], True, False)
        last = mm(ps[:, b, NE:2 * NE], tri, mk[:, 1, :], False, True, sig=True)
        t = vtt(posm, ps[:, b, 0:2 * NE].rearrange("p (t e) -> p t e", t=2), mk, ALU.mult, last)
        bank_free[b] = t
        t_pm = vts(posm, posm, -1.0, None, ALU.add, None, t)
        over = posi[0:1, 0:1]
        m1 = sm[:, 296:297]
        a = vred(m1, sm[:, 160:224], ALU.max, t_pm)
        b = nb()
        a = tr(ps[0:1, b, 0:P], m1, a, bank_free[b], sig=True)
        a = bank_free[b] = vred(sm[0:1, 297:298], ps[0:1, b, 0:P], ALU.max, a)
        t_over = vcopy(over, sm[0:1, 297:298], a, t_pos)
        most = {}

        def load_most(q):
            q.raw(lambda e: most.__setitem__(q, e.value_load(over, min_val=0, max_val=T - 1)), t_over)

        for q in (PE, A, V):
            load_most(q)
        t_S = []
        for t in range(2):
            t_S.append(vtt(S[:, t], bc(iota.unsqueeze(1), [P, NE, CAP]), bc(posm[:, t, :].unsqueeze(2), [P, NE, CAP]),
                           ALU.is_equal, t_pm, t_iota, t_sb))
        b = nb()
        for t in range(2):
            last = tr(ps[0:NE, b, t * P:(t + 1) * P], gate[:, t, :], t_g, bank_free[b], sig=True)
        t_gT = bank_free[b] = vcopy(gT[0:NE, :], ps[0:NE, b, 0:T], last, t_sb)
        t_GT = []
        last_g = None
        for t in range(2):
            t_Sg = [vtt(Sg[:, :, c, :], S[:, t], bc(gate[:, t, :].unsqueeze(2), [P, NE, CAP]), ALU.mult, t_S[t], t_g, last_g, t_sb)
                    for c in range(2)]
            for e in range(0, NE, 4):
                b = nb()
                for j in range(4):
                    last_g = tr(ps[:, b, j * P:(j + 1) * P], Sg[:, e + j].rearrange("p c s -> p (c s)"), t_Sg, bank_free[b],
                                sig=(j == 3))
                o, i = GT[:, e:e + 4, t * P:(t + 1) * P], ps[:, b, :].rearrange("p (a b) -> p a b", a=4)
                bank_free[b] = act(o, i, ACT.Copy, last_g, t_sb) if e % 8 else vcopy(o, i, last_g, t_sb)
                t_GT.append(bank_free[b])

        Y = [[0, 1], [2, 3]]
        GB, LB, DB, TB = 4, 5, 6, 7
        for t in range(2):
            for c in range(2):
                mm(ps[:, Y[t][c], :], gT[0:NE, t * P:(t + 1) * P], bdn[0:NE, c * 512:(c + 1) * 512], True, False,
                   t_gT, t_bdn, bank_free[Y[t][c]])
        t_y0 = PE(lambda e: e.transpose(ps[:, TB, 0:P], ident[:, :], ident[:, :]), bank_free[TB])

        t_xg = {}
        gu_tok = {}

        def gather(j, i, bank):
            dst = xg[j % 2]
            for a in range(2):
                k = 2 * i + a
                for t in range(2):
                    last = mm(ps[:, bank, a * 256:(a + 1) * 256], u[:, t, k * P:(k + 1) * P], S[:, t, 4 * j:4 * j + 4, :],
                              t == 0, t == 1, t_S, bank_free[bank], sig=(t == 1 and a == 1))
            for a in range(2):
                k = 2 * i + a
                bank_free[bank] = act(dst[:, k, :], ps[:, bank, a * 256:(a + 1) * 256], ACT.Copy, last,
                                      [gu_tok[4 * j - 5]] if j >= 2 else t_GT, scale=col("g_moe", k))
            t_xg.setdefault(j, []).append(bank_free[bank])

        for i in range(4):
            gather(0, i, (GB, LB, DB, TB)[i])

        t_act, t_aT, t_yb, t_dn, t_sc2 = {}, {}, {}, {}, {}

        def experts_up(e):
            x = xg[(e // 4) % 2]
            c0 = (e % 4) * CAP
            for half, bank in ((0, GB), (1, LB)):
                for c in range(2):
                    mm(ps[c * 64:c * 64 + 64, bank, :], bc(ident[:, e:e + 1], [P, CAP]),
                       bgu[:, half * D + c * 512:half * D + (c + 1) * 512], True, False, t_bgu, bank_free[bank])
            for k in range(KD):
                w = slot(L_gu[e][k])
                for half, bank in ((0, GB), (1, LB)):
                    for c in range(2):
                        tok = mm(ps[c * 64:c * 64 + 64, bank, :], x[:, k, c0:c0 + CAP],
                                 w[:, half * D + c * 512:half * D + (c + 1) * 512], False, k == KD - 1,
                                 t_xg[e // 4], landed(L_gu[e][k]), sig=(half == 1 and c == 1))
                freed[L_gu[e][k]] = tok
            gu_tok[e] = tok
            tg = vts(glu, ps[:, GB, :], 7.0, None, ALU.min, None, tok, t_y0)
            bank_free[GB] = tg
            t_sg = act(sig, glu, ACT.Sigmoid, tg, scale=1.702)
            tl = vts(lin, ps[:, LB, :], 7.0, -7.0, ALU.min, ALU.max, tok)
            bank_free[LB] = tl
            ta = vstt(lin, lin, 1.0, glu, ALU.add, ALU.mult, tl, tg)
            t_act[e] = vtt(actv, lin, sig, ALU.mult, ta, t_sg, t_aT.get(e - 1))

        def experts_turn(e):
            for j in range(4):
                last = tr(ps[:, TB, j * P:(j + 1) * P], actv[:, j * P:(j + 1) * P], t_act[e], bank_free[TB], sig=(j == 3))
            t_aT[e] = bank_free[TB] = act(actT[e % 2], ps[:, TB, :].rearrange("p (j m) -> p j m", j=4), ACT.Copy, last,
                                          t_dn.get(e - 2))

        def experts_down(e):
            for kk in range(KD):
                w = slot(L_dn[e][kk // 2], (2, D))
                a = actT[e % 2][:, kk % 4, (kk // 4) * 64:(kk // 4) * 64 + 64]
                for c in range(2):
                    tok = mm(ps[c * 64:c * 64 + 64, DB, :], a, w[:, kk % 2, c * 512:(c + 1) * 512], kk == 0, kk == KD - 1,
                             t_aT[e], landed(L_dn[e][kk // 2]), bank_free[DB], sig=(c == 1 and kk % 2 == 1))
                if kk % 2:
                    freed[L_dn[e][kk // 2]] = tok
            t_dn[e] = tok
            t_yb[e] = bank_free[DB] = act(yb[e % 2], ps[:, DB, :], ACT.Copy, tok, t_sc2.get(e - 2))

        def experts_scatter(e):
            for t in range(2):
                for c in range(2):
                    tok = mm(ps[:, Y[t][c], :], GT[c * 64:c * 64 + 64, e, t * P:(t + 1) * P], yb[e % 2][c * 64:c * 64 + 64, :],
                             False, e == NE - 1, t_yb[e], t_GT, sig=(t == 1 and c == 1))
            t_sc2[e] = tok

        for e in range(NE):
            experts_up(e)
            if e // 4 + 1 < NE // 4:
                gather(e // 4 + 1, e % 4, TB)
            if e >= 1:
                experts_down(e - 1)
            experts_turn(e)
            if e >= 1:
                experts_scatter(e - 1)
        experts_down(NE - 1)
        experts_scatter(NE - 1)
        t_h = []
        for t in range(2):
            for c in range(2):
                hs = h[:, t, c * 512:(c + 1) * 512]
                bank_free[Y[t][c]] = vtt(hs, hs, ps[:, Y[t][c], :], ALU.add, t_sc2[NE - 1])
                t_h.append(bank_free[Y[t][c]])

        OP, OA, OV, OD = (Round(sem(f"s_o{n}")) for n in "pavd")
        MORE = T // CAP - 1
        bgo = ar(4096, 2048)
        xo = ar(6144, KD, CAP)
        GTo = ar(6656, T)
        So = ar(6912, 2, CAP)
        Sgo = ar(7040, 2, 2 * CAP)
        tb, gt, tt = (ar(7296 + 2 * MORE * NE * i, 2, MORE * NE) for i in range(3))
        wgu_o = ring[:, 0:8, :]
        wdn_o = ring[:, 8:12, :].rearrange("p s (a n) -> p (s a) n", a=2)
        loop_deps = [t_sc2[NE - 1], t_h]
        s_set = sem("s_set")
        s_end = sem("s_end")

        def prepare(e):
            ins = [e.memset(bgo, 0.0)]
            for r in range(MORE):
                ins.append(e.tensor_scalar(tb[:, :, r * NE:(r + 1) * NE], posm, -float(CAP * (r + 1)), None, ALU.add))
                ins.append(e.tensor_copy(gt[:, :, r * NE:(r + 1) * NE], gate))
            for x in ins:
                x.then_inc(s_set, 1)
            e.wait_ge(s_set, len(ins))

        o_dma = [OD(lambda e, i: e.dma_start(wgu_o, I["w_gu"][0, bass.ds(i % NE, 1), :, :].rearrange(
                     "a (k p) n -> p (a k) n", p=P)), sig=16),
                 OD(lambda e, i: e.dma_start(wdn_o, I["w_dn"][0, bass.ds(i % NE, 1), :, :].rearrange(
                     "a (k p) n -> p (a k) n", p=P)), sig=16),
                 OD(lambda e, i: e.dma_start(bgo[0:1, :], I["b_gu"][0, bass.ds(i % NE, 1), :]), sig=16)][-1]
        oS = []
        for t in range(2):
            a = OV(lambda e, i, t=t: e.tensor_scalar(So[:, t, :], iota, tb[:, t, 0:1], None, ALU.is_equal), o_dma)
            oS.append(a)
            for c in range(2):
                oS.append(OV(lambda e, i, t=t, c=c: e.tensor_scalar(Sgo[:, t, c * CAP:(c + 1) * CAP], So[:, t, :],
                                                                    gt[:, t, 0:1], None, ALU.mult), a))
        for x in (tb, gt):
            a = OV(lambda e, i, x=x: e.tensor_copy(tt[:, :, 0:MORE * NE - 1], x[:, :, 1:MORE * NE]), oS)
            oS = [OV(lambda e, i, x=x: e.tensor_copy(x[:, :, 0:MORE * NE - 1], tt[:, :, 0:MORE * NE - 1]), a)]

        def omm(o, l, r, start, stop, *waits, sig=0):
            return OP(lambda e, i: e.matmul(o, l, r, start=start, stop=stop), *waits, sig=sig)

        for k in range(KD):
            for t in range(2):
                a = omm(ps[:, GB, k * CAP:(k + 1) * CAP], u[:, t, k * P:(k + 1) * P], So[:, t, :], t == 0, t == 1, oS,
                        sig=int(k == KD - 1 and t == 1))
        ox = [OA(lambda e, i, k=k: e.activation(xo[:, k, :], ps[:, GB, k * CAP:(k + 1) * CAP], ACT.Copy,
                                                scale=col("g_moe", k)), a) for k in range(KD)]
        for t in range(2):
            a = OP(lambda e, i, t=t: e.transpose(ps[:, DB, t * P:(t + 1) * P], Sgo[:, t, :], ident[:, :]), oS, sig=t)
        oG = OA(lambda e, i: e.activation(GTo, ps[:, DB, 0:T], ACT.Copy), a)
        for half, bank in ((0, GB), (1, LB)):
            for c in range(2):
                w0 = half * D + c * 512
                omm(ps[c * 64:c * 64 + 64, bank, :], bc(ident[:, 0:1], [P, CAP]), bgo[:, w0:w0 + 512], True, False, ox, o_dma)
                for k in range(KD):
                    a = omm(ps[c * 64:c * 64 + 64, bank, :], xo[:, k, :], wgu_o[:, k, w0:w0 + 512], False, k == KD - 1,
                            sig=int(half == 1 and c == 1 and k == KD - 1))
        g = OV(lambda e, i: e.tensor_scalar(glu, ps[:, GB, :], 7.0, None, ALU.min), a)
        sg = OA(lambda e, i: e.activation(sig, glu, ACT.Sigmoid, scale=1.702), g)
        a = OV(lambda e, i: e.tensor_scalar(lin, ps[:, LB, :], 7.0, -7.0, ALU.min, ALU.max), a)
        a = OV(lambda e, i: e.scalar_tensor_tensor(out=lin, in0=lin, scalar=1.0, in1=glu, op0=ALU.add, op1=ALU.mult), a, g)
        a = OV(lambda e, i: e.tensor_tensor(actv, lin, sig, ALU.mult), a, sg)
        for j in range(4):
            a = OP(lambda e, i, j=j: e.transpose(ps[:, TB, j * P:(j + 1) * P], actv[:, j * P:(j + 1) * P], ident[:, :]), a,
                   sig=int(j == 3)) if j == 0 else OP(
                       lambda e, i, j=j: e.transpose(ps[:, TB, j * P:(j + 1) * P], actv[:, j * P:(j + 1) * P], ident[:, :]),
                       sig=int(j == 3))
        oT = OA(lambda e, i: e.activation(actT[0], ps[:, TB, :].rearrange("p (j m) -> p j m", j=4), ACT.Copy), a)
        for c in range(2):
            for kk in range(KD):
                a = omm(ps[c * 64:c * 64 + 64, DB, :], actT[0][:, kk % 4, (kk // 4) * 64:(kk // 4) * 64 + 64],
                        wdn_o[:, kk, c * 512:(c + 1) * 512], kk == 0, kk == KD - 1, oT, oG,
                        sig=int(c == 1 and kk == KD - 1))
        oy = OA(lambda e, i: e.activation(yb[0], ps[:, DB, :], ACT.Copy), a)
        for t in range(2):
            for c in range(2):
                a = omm(ps[:, Y[t][c], :], GTo[c * 64:c * 64 + 64, t * P:(t + 1) * P], yb[0][c * 64:c * 64 + 64, :], True, True,
                        oy, oG, sig=int(t == 1 and c == 1))
        for t in range(2):
            for c in range(2):
                hs = h[:, t, c * 512:(c + 1) * 512]
                a_h = OV(lambda e, i, hs=hs, t=t, c=c: e.tensor_tensor(hs, hs, ps[:, Y[t][c], :], ALU.add), a)
        OD(lambda e, i: e.sem_inc(s_end, 1), (OV, OV.n), sig=0)

        def rounds(q, r, setup=lambda e: e.wait_ge(s_set, 1 + 2 * MORE)):
            def body(e):
                with e.If(most[q] >= CAP):
                    for s_, v in flat(loop_deps):
                        e.wait_ge(s_, v)
                    setup(e)
                    with e.Fori(0, MORE * NE) as i:
                        r.emit(e, i)

            q.raw(body)

        rounds(PE, OP)
        rounds(A, OA)
        rounds(V, OV, prepare)
        t_h = [V(lambda e: e.memset(sm[:, 298:299], 0.0))]
        t_pend = PE(lambda e: e.transpose(ps[0:1, TB, 0:P], m1, ident[:, :]), bank_free[TB])
        t_aend = A(lambda e: e.activation(sm[:, 299:300], m1, ACT.Copy))
        t_end = [t_h, t_pend, t_aend]
        bank_free[TB] = t_pend
        if stop == "moe":
            done = finish(t_h)
            return run()

        prow2 = ar(12288, 2, 256)
        pT = ar(12800, 2, T)
        gfin, gmix, gffn = (ar(13312 + 1024 * i, 1024) for i in range(3))
        t_moe = [gu_tok[NE - 1]]
        t_p = dma(G, "d_p", prow2, I["p"][0, 0].rearrange("(t p) d -> p t d", p=P), t_moe)
        t_gb = [dma(G, f"d_gb{i}", g, bc(src, [P, D]), t_moe) for i, (g, src) in enumerate(
            ((gfin, I["g_final"].rearrange("(a d) -> a d", a=1)), (gmix, I["g_post_mix_2"]), (gffn, I["g_post_ffn_2"])))]
        Bb = ar(0, 3072)
        B0, B1 = halves(Bb)
        flatskew = skew.rearrange("h p m -> h (p m)")

        def skewed(off, n):
            return bass.AP(skew.tensor, off, [[511, P], [P * 512, 8], [1, n]])

        t_B = [dma(G, "d_B0", B0, skewed(255, P), t_moe, t_skew),
               dma(G, "d_B1", B1, skewed(127, T), t_moe, t_skew)]
        wbd = [ar(3072 + 512 * i, 4, P) for i in range(2)]
        t_wz = V(lambda e: e.memset(ar(3072, 1024), 0.0), t_moe)
        t_wbd = []
        for i, n in enumerate(("w_r_2", "w_i_2")):
            v = I[n][0].rearrange("(j s) c d -> s c j d", s=2)
            for s2 in range(2):
                t_wbd.append(dma(G, f"d_{n}{s2}", wbd[i][64 * s2:64 * s2 + 64, :, 64 * s2:64 * s2 + 64], v[s2], t_wz))

        t_u = norm_rows(h, u, u, [(0, D)], t_h, t_end)
        t_uT = to_columns(u, uT, 0, KD, lambda k: col("g_ple", k), t_u, t_end)
        b = nb()
        for k in range(2):
            for t in range(2):
                last = tr(ps[:, b, k * T + t * P:k * T + (t + 1) * P], prow2[:, t, k * P:(k + 1) * P], t_p, bank_free[b],
                          sig=(k == 1 and t == 1))
        t_pT = bank_free[b] = act(pT, ps[:, b, :].rearrange("p (a b) -> p a b", a=2), ACT.Copy, last)
        bs, last = rows_product(uT, KD, L_pg, 2, 1024, t_uT)
        bp, last2 = rows_product(pT, 2, [L_pp], 2, 1024, t_pT)
        t_h = []
        for t in range(2):
            for n in range(2):
                us, hs = u[:, t, n * 512:(n + 1) * 512], h[:, t, n * 512:(n + 1) * 512]
                a = bank_free[bs[t][n]] = act(us, ps[:, bs[t][n], :], ACT.Sigmoid, last, t_uT)
                a = bank_free[bp[t][n]] = vtt(us, us, ps[:, bp[t][n], :], ALU.mult, a, last2)
                t_h.append(vtt(hs, hs, us, ALU.add, a))
        junk = ar(4096, 2, D)
        t_r = rstd([(h[:, t, :], junk[:, t, :], D) for t in range(2)], t_h, t_end)
        t_h = [vstt(h[:, t, :], h[:, t, :], rs[:, t:t + 1], gfin, ALU.mult, ALU.mult, t_r, t_gb) for t in range(2)]
        if stop == "ple":
            done = finish(t_h)
            return run()

        t_u = norm_rows(h, u, u, [(0, D)], t_h)
        t_uT = to_columns(u, uT, 0, KD, lambda k: col("g_pre_mix_2", k), t_u, [last])
        S2 = ar(4096, 3072)
        PT3 = ar(7168, 3072)
        q2, k2 = ar(10240, 4, T), ar(11264, 4, T)
        v2 = ar(16384, 2, 512)
        xr, gr, xc = (ar(17408 + 1024 * i, 4, T) for i in range(3))
        t_moe = [t_end, V.last(), A.last()]
        tq = []
        for half, dst in ((0, q2), (1, k2)):
            for j in range(0, 4, 2):
                b = nb()
                for m in range(2):
                    tk = columns_product(uT, L2_qk, 2, 1024, half * 4 + j + m, ps[:, b, m * T:(m + 1) * T],
                                         [t_uT, bank_free[b]], True)
                bank_free[b] = act(dst[:, j:j + 2, :], ps[:, b, :].rearrange("p (a b) -> p a b", a=2), ACT.Copy, tk, t_moe)
                tq.append(bank_free[b])
        for s in L2_qk:
            freed[s] = tk
        bs, last = rows_product(uT, KD, L2_v, 4, 512, t_uT)
        t_v = []
        for t in range(2):
            bank_free[bs[t][0]] = act(v2[:, t, :], ps[:, bs[t][0], :], ACT.Copy, last, t_moe)
            t_v.append(bank_free[bs[t][0]])
        b0, b1, last = pair_scores(q2, k2, tq)
        S0, S1 = halves(S2)
        B0v = B0.rearrange("p (i s) k -> p s i k", s=2)
        B1v = B1.rearrange("p (i s) k -> p s i k", s=2)
        t_s = []
        for par in range(2):
            bank_free[b0[par]] = vstt(S0[:, 4 * par:4 * par + 4, :], ps[:, b0[par], :].rearrange("p (a b) -> p a b", a=4),
                                      SBS, B0v[:, par], ALU.mult, ALU.add, last, t_B, t_r)
            t_s.append(bank_free[b0[par]])
            for i in range(2):
                b = b1[par][i]
                bank_free[b] = vstt(S1[:, 4 * par + 2 * i:4 * par + 2 * i + 2, :],
                                    ps[:, b, :].rearrange("p (a b) -> p a b", a=2), SBS,
                                    B1v[:, par, 2 * i:2 * i + 2], ALU.mult, ALU.add, last, t_B, t_r)
                t_s.append(bank_free[b])
        tx = []
        for half, dst in ((0, xr), (1, gr)):
            for j in range(0, 4, 2):
                b = nb()
                for m in range(2):
                    tk = columns_product(uT, L2_xg, 2, 1024, half * 4 + j + m, ps[:, b, m * T:(m + 1) * T],
                                         [t_uT, bank_free[b]], True)
                bank_free[b] = act(dst[:, j:j + 2, :], ps[:, b, :].rearrange("p (a b) -> p a b", a=2), ACT.Copy, tk, t_moe)
                tx.append(bank_free[b])
        for s in L2_xg:
            freed[s] = tk
        t_proj = tk
        t_e, t_r = softmax(S2, t_s)
        t_xc = []
        for c in range(4):
            a = vts(xc[:, c, :], xr[:, c, :], col("w_conv_lru_2", 12 + c), col("b_conv_lru_2", c), ALU.mult, ALU.add, tx, t_moe)
            for d in (1, 2, 3):
                a = vstt(xc[:, c, d:], xr[:, c, 0:T - d], col("w_conv_lru_2", (3 - d) * 4 + c), xc[:, c, d:],
                         ALU.mult, ALU.add, a)
            t_xc.append(a)
        mixT = ar(0, KD, T)
        uf = u[:, :, :].rearrange("p t d -> p (t d)")
        rg, ig = (uTf[:, 1024 * i:1024 * i + 1024].rearrange("p (c t) -> p c t", c=4) for i in range(2))
        av, tv_ = (uf[:, 1024 * i:1024 * i + 1024].rearrange("p (c t) -> p c t", c=4) for i in range(2))
        lam0, lam1 = sm[:, 288:292], sm[:, 292:296]
        lam = cols[:, col0[0] + rows["lam_2"][1]:col0[0] + rows["lam_2"][1] + 4]
        a = act(lam0, lam, ACT.Abs, t_cols)
        a = act(lam0, lam0, ACT.Exp, a, scale=-1.0)
        a = act(lam0, lam0, ACT.Ln, a, bias=1.0)
        b_ = vts(lam1, lam, -1.0, 0.0, ALU.mult, ALU.max, t_cols)
        a = vtt(lam0, lam0, lam1, ALU.add, a, b_)
        t_lam = vts(lam0, lam0, -8.0, None, ALU.mult, None, a)

        bo, last = weigh(S2, lambda hd: 4 * (hd % 2) + hd // 2, PT3, v2, [t_e], [t_r], t_v)
        o2 = tv_.rearrange("p c t -> p (c t)").rearrange("p (t d) -> p t d", t=2)
        t_o = []
        for t in range(2):
            rv = rsum[:, 8 * t:8 * t + 8].rearrange("p (s i) -> p i s", s=2)
            o = o2[:, t, :].rearrange("p (i s d) -> p i s d", i=4, s=2)
            i = ps[:, bo[t], :].rearrange("p (i s d) -> p i s d", i=4, s=2)
            bank_free[bo[t]] = vtt(o, i, bc(rv.unsqueeze(3), [P, 4, 2, 64]), ALU.mult, last, t_r, t_uT)
            t_o.append(bank_free[bo[t]])
        t_aT2 = []
        for k in range(0, 4, 2):
            b = nb()
            for j in range(2):
                for t in range(2):
                    last_a = tr(ps[:, b, j * T + t * P:j * T + (t + 1) * P], o2[:, t, (k + j) * P:(k + j + 1) * P], t_o,
                                bank_free[b], sig=(j == 1 and t == 1))
            bank_free[b] = act(mixT[:, k:k + 2, :], ps[:, b, :].rearrange("p (a b) -> p a b", a=2), ACT.Copy, last_a, t_s)
            t_aT2.append(bank_free[b])
        t_gr = []
        for g, (dst, bias) in enumerate(((rg, "b_r_2"), (ig, "b_i_2"))):
            for c in range(4):
                b = nb()
                tk = mm(ps[:, b, 0:T], wbd[g][:, c, :], xc[:, c, :], True, True, t_wbd, t_xc, bank_free[b], sig=True)
                bank_free[b] = act(dst[:, c, :], ps[:, b, 0:T], ACT.Sigmoid, tk, t_proj, bias=col(bias, c))
                t_gr.append(bank_free[b])
        ta = [vts(rg[:, c, :], rg[:, c, :], lam0[:, c:c + 1], None, ALU.mult, None, t_gr, t_lam) for c in range(4)]
        tb_ = vtt(ig, ig, xc, ALU.mult, t_gr)
        t_a = act(av, rg, ACT.Exp, ta, t_uT)
        t_t = act(tv_, rg, ACT.Tanh, ta, last_a, scale=-1.0)
        a = vts(rg, tv_, 1.0, None, ALU.add, None, t_t, t_a)
        a = vrecip(rg, rg, a)
        a = vstt(tv_, tv_, 2.0, rg, ALU.mult, ALU.mult, a)
        a = act(tv_, tv_, ACT.Sqrt, a)
        a = vtt(ig, ig, tv_, ALU.mult, a, tb_)
        t_hh = []
        for c in range(4):
            t_hh.append(V(lambda e, c=c: e.tensor_tensor_scan(xr[:, c, :], av[:, c, :], ig[:, c, :], 0.0, ALU.mult, ALU.add),
                          a, t_a, t_xc))
        t_gl = act(gr, gr, ACT.Gelu_apprx_tanh, tx)
        t_lr = vtt(mixT[:, 4:8, :], xr, gr, ALU.mult, t_hh, t_gl, t_s)

        bs, last = rows_product(mixT, KD, L2_o, 2, 1024, [t_aT2, t_lr])
        t_m = []
        for t in range(2):
            for n in range(2):
                b = bs[t][n]
                us = u[:, t, n * 512:(n + 1) * 512]
                bank_free[b] = act(us, ps[:, b, :], ACT.Copy, last, t_hh, a) if n else vcopy(us, ps[:, b, :], last, t_hh)
                t_m.append(bank_free[b])
        junk = PT3[:, 0:2048].rearrange("p (t d) -> p t d", t=2)

        def add_normed(gb, waits):
            t_r = rstd([(u[:, t, :], junk[:, t, :], D) for t in range(2)], waits)
            toks = []
            for t in range(2):
                a = vstt(u[:, t, :], u[:, t, :], rs[:, t:t + 1], gb, ALU.mult, ALU.mult, t_r, t_gb)
                toks.append(vtt(h[:, t, :], h[:, t, :], u[:, t, :], ALU.add, a))
            return toks

        t_h = add_normed(gmix, t_m)
        if stop == "mix":
            done = finish(t_h)
            return run()

        t_u = norm_rows(h, u, u, [(0, D)], t_h)
        t_uT = to_columns(u, uT, 0, KD, lambda k: col("g_pre_ffn_2", k), t_u, [V.last()])
        fT = ar(4096, 22, T)
        tmp = [ar(10240 + 256 * i, T) for i in range(8)]
        t_tmp = [None] * 8
        t_f = []

        def taps(c):
            return col("w_conv_ffn_2", c), col("w_conv_ffn_2", 44 + c), col("w_conv_ffn_2b", c), col("b_conv_ffn_2", c)

        def conv_tile(s, m, c, y, free):
            b = nb()
            w = slot(s, (8, 256))
            for k in range(KD):
                tok = mm(ps[:, b, 0:T], w[:, k, m * P:(m + 1) * P], uT[:, k, :], k == 0, k == KD - 1, t_uT, landed(s),
                         bank_free[b], sig=(k == KD - 1))
            freed[s] = tok
            w0, w1, w2_, bb = taps(c)
            a = act(y, ps[:, b, 0:T], ACT.Identity, tok, free, scale=w2_, bias=bb)
            a = vstt(y[:, 1:], ps[:, b, 0:T - 1], w1, y[:, 1:], ALU.mult, ALU.add, a)
            bank_free[b] = vstt(y[:, 2:], ps[:, b, 0:T - 2], w0, y[:, 2:], ALU.mult, ALU.add, a)
            return bank_free[b]

        t_pv = [last, PE.last()]
        for i in range(11):
            pend = []
            for half in range(2):
                for m in range(2):
                    c = 2 * i + m
                    y = (4 * (i % 2)) + 2 * half + m
                    pend.append(conv_tile(L2_up[2 * i + half], m, 22 * half + c, tmp[y], [t_tmp[y], t_pv, t_h]))
            for m in range(2):
                y = 4 * (i % 2) + m
                a = act(tmp[y + 2], tmp[y + 2], ACT.Gelu_apprx_tanh, pend[2 + m])
                t = vtt(fT[:, 2 * i + m, :], tmp[y], tmp[y + 2], ALU.mult, a, pend[m], t_pv)
                t_tmp[y] = t_tmp[y + 2] = t
                t_f.append(t)

        bs = [[nb(), nb()], [nb(), nb()]]
        for k in range(22):
            s = L2_dn[k // 2]
            w = slot(s, (2, 1024))
            for t in range(2):
                for n in range(2):
                    last = mm(ps[:, bs[t][n], :], fT[:, k, t * P:(t + 1) * P], w[:, k % 2, n * 512:(n + 1) * 512],
                              k == 0, k == 21, t_f[k], landed(s), bank_free[bs[t][n]], sig=(t == 1 and n == 1))
            freed[s] = last
        t_m = []
        for t in range(2):
            for n in range(2):
                b = bs[t][n]
                us = u[:, t, n * 512:(n + 1) * 512]
                bank_free[b] = act(us, ps[:, b, :], ACT.Copy, last, t_uT) if n else vcopy(us, ps[:, b, :], last, t_uT)
                t_m.append(bank_free[b])
        junk = ar(10240, 2, D)
        t_h = add_normed(gffn, t_m + t_f)
        done = finish(t_h)
        run()


_INS = ['x', 'p', 'positions', 'w_in', 'g_attn', 'g_cq', 'w_uq', 'g_ckv', 'w_ukv', 'g_out_mla', 'g_out_sb', 'w_o', 'g_moe',
        'w_router', 'b_router', 'w_gu', 'b_gu', 'w_dn', 'b_dn', 'g_ple', 'w_ple_gate', 'w_ple_proj', 'g_final',
        'g_pre_mix_2', 'w_in_2', 'rel_bias_2', 'w_conv_lru_2', 'b_conv_lru_2', 'w_r_2', 'b_r_2', 'w_i_2', 'b_i_2',
        'lam_2', 'w_out_2', 'g_post_mix_2', 'g_pre_ffn_2', 'w_up_2', 'w_conv_ffn_2', 'b_conv_ffn_2', 'w_down_2',
        'g_post_ffn_2']


def kernel(**inputs):
    import concourse.bacc as _bacc
    from concourse.bass_utils import run_bass_kernel_spmd as _run

    nc = _bacc.Bacc("TRN2", target_bir_lowering=False, num_devices=1)
    given = {name: np.ascontiguousarray(inputs[name]) for name in _INS}
    given["c_bucket"] = bucket_table()
    given["c_inv_freq"] = inv_freq_table()
    arrays, aps = {}, {}
    for name, a in given.items():
        arrays[f"in_{name}_dram"] = a
        aps[name] = nc.dram_tensor(f"in_{name}_dram", a.shape, mybir.dt.from_np(a.dtype), kind="ExternalInput").ap()
    out = nc.dram_tensor("out_0_dram", (1, T, D), F32, kind="ExternalOutput").ap()
    build_program(nc, aps, out)
    r = _run(nc, [arrays], core_ids=[0])
    return r.results[0]["out_0_dram"]
```

```python
import math
from contextlib import ExitStack

import numpy as np

import concourse.bass as bass
from concourse import mybir

F32 = mybir.dt.float32
F32R = mybir.dt.float32r
I32 = mybir.dt.int32
U32 = mybir.dt.uint32
ALU = mybir.AluOpType
ACT = mybir.ActivationFunctionType
AX = mybir.AxisListType

P = 128
T = 256
D = 1024
KD = D // P
NE = 32
CAP = 64
NSLOT = 8
SLOTW = 2048
NEG = -1.0e30
EPS = 1e-6
TWO_PI = 2.0 * math.pi
C1 = 6.28125
C2 = float(np.float32(np.floor((TWO_PI - C1) * 2.0 ** 21) / 2.0 ** 21))
C3 = TWO_PI - C1 - C2
MAGIC = 12582912.0


class Queue:

    def __init__(self, sem):
        self.sem, self.items, self.n = sem, [], 0

    def __call__(self, fn, *waits, sig=True):
        self.items.append((flat(waits), fn, sig))
        self.n += sig
        return (self.sem, self.n) if sig else None

    def last(self):
        return (self.sem, self.n)

    def emit(self, eng):
        seen = {}
        for waits, fn, sig in self.items:
            for sem, v in waits:
                if seen.get(sem, 0) < v:
                    eng.wait_ge(sem, v)
                    seen[sem] = v
            ins = fn(eng)
            if sig is True:
                ins.then_inc(self.sem, 1)

    def raw(self, fn, *waits):
        self.items.append((flat(waits), fn, False))


class Round:

    def __init__(self, sem):
        self.sem, self.items, self.n = sem, [], 0

    def __call__(self, fn, *waits, sig=1):
        self.items.append((flat(waits), fn, sig))
        self.n += sig
        return (self, self.n)

    def emit(self, eng, i):
        seen = {}
        for waits, fn, sig in self.items:
            for q, v in waits:
                if seen.get(q, 0) < v:
                    eng.wait_ge(q.sem, i * q.n + v)
                    seen[q] = v
            ins = fn(eng, i)
            if sig:
                ins.then_inc(self.sem, sig)


def flat(waits):
    out = []
    for w in waits:
        if w is None:
            continue
        if isinstance(w, list):
            out += flat(w)
        else:
            out.append(w)
    return out


def bucket_table():
    oh = np.zeros((33, 512), np.float32)
    for m in range(512):
        n = 255 - m
        if n < 0:
            oh[32, m] = 1.0
            continue
        b = n if n < 16 else min(31, 16 + int(math.log(n / 16.0) / math.log(128 / 16) * 16 + 1e-9))
        oh[b, m] = 1.0
    return oh


def inv_freq_table():
    f = 10000.0 ** (-np.arange(0, 32, 2, dtype=np.float64) / 32)
    return f.astype(np.float32).reshape(1, 16)


def build_program(nc, I, out, stop=None):
    ctx = ExitStack()
    with ctx:
        def sb(name, shape, dt=F32):
            return ctx.enter_context(nc.sbuf_tensor(name, shape, dt))

        def sem(name):
            return ctx.enter_context(nc.semaphore(name))

        def bc(ap, shape):
            return ap.broadcast_to(shape)

        ring = sb("ring", [P, NSLOT, SLOTW])
        h = sb("h", [P, 2, D])
        u = sb("u", [P, 2, D])
        arena = sb("arena", [P, 18432])
        W = sb("W", [P, 2, 2, SLOTW], F32R)
        X = sb("X", [P, 2, KD, T], F32R)
        xin = (X[:, 0], X[:, 1])
        ident = sb("ident", [P, P])
        cols = sb("cols", [P, 264])
        msk = sb("msk", [P, 3, T])
        sm = sb("sm", [P, 320])
        wr = sb("wr", [P, KD, NE])
        posi = sb("posi", [P, 2], I32)
        ps = ctx.enter_context(nc.psum_tensor("ps", [P, 8, 512], F32))
        skew = nc.dram_tensor("skew", [8, P, 512], F32, kind="Internal").ap()

        PE = Queue(sem("s_pe"))
        A = Queue(sem("s_act"))
        V = Queue(sem("s_dve"))
        G = Queue(sem("s_pool"))
        SP = Queue(sem("s_sp"))
        slot_sem = [sem(f"s_slot{i}") for i in range(NSLOT + 3)]

        def ar(off, *shape):
            n = int(np.prod(shape))
            v = arena[:, off:off + n]
            if len(shape) == 2:
                v = v.rearrange("p (a b) -> p a b", a=shape[0])
            elif len(shape) == 3:
                v = v.rearrange("p (a b c) -> p a b c", a=shape[0], b=shape[1])
            return v

        def dma(q, name, dst, src, *waits):
            s = sem(name)
            q(lambda e: e.dma_start(dst, src).then_inc(s, 16), *waits, sig=False)
            return (s, 16)

        places = [ring[:, i, :] for i in range(NSLOT)] + [ar(12288 + 2048 * i, 2048) for i in range(3)]
        loads, freed = [], {}
        turn = {"order": list(range(NSLOT)), "at": 0}
        held, count = {}, [0] * len(places)

        def take_turns(order):
            turn["order"], turn["at"] = order, 0

        def load(src, cols_n, **shape):
            n = len(loads)
            i = turn["order"][turn["at"] % len(turn["order"])]
            turn["at"] += 1
            dst = places[i][:, 0:cols_n]
            if shape:
                dst = dst.rearrange("p (a b) -> p a b", **shape)
            count[i] += 1
            loads.append((dst, src, i, held.get(i), count[i]))
            held[i] = n
            return n

        def slot(n, a=None):
            v = places[loads[n][2]]
            return v if a is None else v[:, 0:a[0] * a[1]].rearrange("p (a b) -> p a b", a=a[0])

        def landed(n):
            return (slot_sem[loads[n][2]], 16 * loads[n][4])

        def mm(o, l, r, start, stop, *waits, sig=False):
            return PE(lambda e: e.matmul(o, l, r, start=start, stop=stop), *waits, sig=sig)

        def tr(o, i, *waits, sig=False):
            n = i.shape[0]
            return PE(lambda e: e.transpose(o, i, ident[0:n, 0:n]), t_ident, *waits, sig=sig)

        def act(o, i, f, *waits, **kw):
            return A(lambda e: e.activation(o, i, f, **kw), *waits)

        def vcopy(o, i, *waits):
            return V(lambda e: e.tensor_copy(o, i), *waits)

        def vts(o, i, s1, s2, op0, op1, *waits):
            if op1 is None:
                return V(lambda e: e.tensor_scalar(o, i, s1, None, op0), *waits)
            return V(lambda e: e.tensor_scalar(o, i, s1, s2, op0, op1), *waits)

        def vtt(o, a, b, op, *waits):
            return V(lambda e: e.tensor_tensor(o, a, b, op), *waits)

        def vstt(o, a, s, b, op0, op1, *waits):
            return V(lambda e: e.scalar_tensor_tensor(out=o, in0=a, scalar=s, in1=b, op0=op0, op1=op1), *waits)

        def vred(o, i, op, *waits):
            return V(lambda e: e.tensor_reduce(o, i, AX.X, op), *waits)

        def vrecip(o, i, *waits):
            return V(lambda e: e.reciprocal(o, i), *waits)

        bank_free = [None] * 8
        state = {"bank": 0, "pair": 0, "primed": 299}

        def nb():
            b = state["bank"]
            state["bank"] = (b + 1) % 8
            return b

        t1 = G(lambda e: e.memset(ident[:, :], 0.0))
        t_ident = G(lambda e: e.affine_select(out=ident[:, :], in_=ident[:, :], compare_op=ALU.not_equal, fill=1.0,
                                              base=0, pattern=[[-1, P]], channel_multiplier=1), t1)
        t1 = G(lambda e: e.memset(msk[:, 0:2, :], 0.0))
        t2 = G(lambda e: e.memset(msk[:, 2, :], -1.0))
        t3 = G(lambda e: e.affine_select(out=msk[:, 0, :], in_=msk[:, 0, :], compare_op=ALU.is_ge, fill=NEG, base=P,
                                         pattern=[[-1, T]], channel_multiplier=1), t1, t2)
        t3 = G(lambda e: e.affine_select(out=msk[:, 1, :], in_=msk[:, 1, :], compare_op=ALU.is_gt, fill=NEG, base=P,
                                         pattern=[[-1, T]], channel_multiplier=1))
        t_msk = G(lambda e: e.affine_select(out=msk[:, 2, :], in_=msk[:, 2, :], compare_op=ALU.is_gt, fill=0.0, base=P,
                                            pattern=[[-1, T]], channel_multiplier=1))
        iota = sm[:, 48:112]
        t_iota = G(lambda e: e.iota(iota, [[1, CAP]], base=0, channel_multiplier=0,
                                    allow_small_or_imprecise_dtypes=True))

        onec = sm[:, 152:153]
        t_one = G(lambda e: e.memset(onec, 1.0))

        xv = I["x"][0].rearrange("(t p) d -> p t d", p=P)
        t_x = [dma(SP, f"d_x{t}", h[:, t, :], xv[:, t, :]) for t in range(2)]
        stage = ar(15360, 4, P)
        rows = {}
        small = [[], [], [], []]
        used = [0, 0, 0, 0]

        def rowload(tile, name, src, n, q=G):
            r = used[tile]
            rows[name] = (tile, r)
            small[tile].append(dma(q, f"d_{name}", stage[r:r + n, tile, :], src))
            used[tile] = r + n

        def vec(name, k):
            return I[name].rearrange("a (k p) -> (a k) p", p=P)

        rowload(3, "g_attn", vec("g_attn", 8), 8, SP)
        NX = len(SP.items)
        for name, k in (("g_cq", 3), ("g_ckv", 2), ("g_out_mla", 4), ("g_out_sb", 4), ("g_moe", 8),
                        ("g_ple", 8), ("g_pre_mix_2", 8), ("b_conv_lru_2", 4), ("b_r_2", 4), ("b_i_2", 4),
                        ("lam_2", 4), ("g_pre_ffn_2", 8)):
            rowload(0, name, vec(name, k), k)
        rowload(0, "w_conv_lru_2", I["w_conv_lru_2"].rearrange("a j (k p) -> (a j k) p", p=P), 16)
        col0 = (0, 88, 176, 77)

        def col(name, k=0):
            tile, r = rows[name]
            c = col0[tile] + r + k
            return cols[:, c:c + 1]

        t_pos = [dma(G, f"d_pos{t}", posi[:, t:t + 1], I["positions"][0, t * P:(t + 1) * P].rearrange("(p a) -> p a", a=1))
                 for t in range(2)]
        invf = sm[:, 0:16]
        t_inv = dma(G, "d_inv", invf, bc(I["c_inv_freq"], [P, 16]))
        rowload(1, "w_conv_ffn_2", I["w_conv_ffn_2"][0, 0:2].rearrange("j (k p) -> (j k) p", p=P), 88)
        rowload(2, "w_conv_ffn_2b", I["w_conv_ffn_2"][0, 2:3].rearrange("j (k p) -> (j k) p", p=P), 44)
        rowload(2, "b_conv_ffn_2", vec("b_conv_ffn_2", 44), 44)
        brt = sm[:, 16:48]
        t_brt = dma(G, "d_brt", brt, bc(I["b_router"], [P, 32]))
        oht = ar(8192, 512)[0:33, :]
        rel = ar(8704, 16)[0:33, 0:8]
        t_rel0 = V(lambda e: e.memset(ar(8704, 16)[:, :], NEG))
        t_oht = dma(G, "d_oht", oht, I["c_bucket"])
        t_rel = dma(G, "d_rel", rel[0:32, :], I["rel_bias_2"], t_rel0)
        t_wr = dma(G, "d_wr", wr[:, :, :], I["w_router"][0].rearrange("(k p) e -> p k e", p=P))

        def stage_columns(tile):
            n = used[tile]
            b = nb()
            t = tr(ps[:, b, 0:n], stage[0:n, tile, :], small[tile], bank_free[b], sig=True)
            bank_free[b] = vcopy(cols[:, col0[tile]:col0[tile] + n], ps[:, b, 0:n], t)
            return bank_free[b]

        def kload(src, k0, nk, c0, nc_):
            return load(src[k0 * P:(k0 + nk) * P, c0:c0 + nc_].rearrange("(k p) n -> p k n", p=P), nk * nc_, a=nk)

        def cload(src, c0):
            return load(src[:, c0:c0 + 256].rearrange("(k p) n -> p k n", p=P), 2048, a=KD)

        w_in, w_o = I["w_in"][0], I["w_o"][0]
        L_a = [kload(w_in, k, n, 0, 672) for k, n in ((0, 3), (3, 3), (6, 2))]
        L_qk = [cload(w_in, 672 + 256 * j) for j in range(4)]
        L_v = [kload(w_in, 4 * j, 4, 1696, 512) for j in range(2)]
        L_uq = [kload(I["w_uq"][0], 0, 2, 0, 768), kload(I["w_uq"][0], 2, 1, 0, 768)]
        L_ukv = kload(I["w_ukv"][0], 0, 2, 0, 1024)
        L_o = {j: kload(w_o, 2 * j, 2, 0, 1024) for j in (2, 3, 0, 1)}
        L_gu, L_dn = {}, {}

        def load_gu(e):
            L_gu[e] = [load(I["w_gu"][0, e, k * P:(k + 1) * P, :], 2048) for k in range(KD)]

        def load_dn(e):
            L_dn[e] = [kload(I["w_dn"][0, e], 2 * j, 2, 0, 1024) for j in range(4)]

        take_turns([0, 1, 2, 3, 8, 9, 10, 4, 5, 6, 7])
        load_gu(0)
        for e in range(1, NE):
            load_gu(e)
            load_dn(e - 1)
        load_dn(NE - 1)
        first = (turn["at"]) % 11
        take_turns([i for i in turn["order"][first:] + turn["order"][:first] if i < NSLOT])
        L_pp = kload(I["w_ple_proj"][0], 0, 2, 0, 1024)
        L_pg = [kload(I["w_ple_gate"][0], 2 * j, 2, 0, 1024) for j in range(4)]
        w2 = I["w_in_2"][0]
        L2_qk = [cload(w2, 256 * j) for j in range(4)]
        L2_xg = [cload(w2, 1536 + 256 * j) for j in range(4)]
        L2_v = [kload(w2, 4 * j, 4, 1024, 512) for j in range(2)]
        L2_o = [kload(I["w_out_2"][0], 2 * j, 2, 0, 1024) for j in range(4)]
        wup = I["w_up_2"][0]
        L2_up = [cload(wup, half * 2816 + i * 256) for i in range(11) for half in range(2)]
        L2_dn = [kload(I["w_down_2"][0], 2 * j, 2, 0, 1024) for j in range(11)]

        ss = sm[:, 112:116]
        rs = sm[:, 116:120]
        rn = [0]

        def rstd(parts, *waits, c0=0):
            ts = []
            for c, (src, junk, n, *own) in enumerate(parts, c0):
                ts.append(act(junk, src, ACT.Square, *waits, own, accum_out=ss[:, c:c + 1]))
            tv = []
            for c, (src, junk, n, *own) in enumerate(parts, c0):
                tv.append(vts(rs[:, c:c + 1], ss[:, c:c + 1], 1.0 / n, EPS, ALU.mult, ALU.add, ts[c - c0]))
            n = len(parts)
            t = act(rs[:, c0:c0 + n], rs[:, c0:c0 + n], ACT.Sqrt, tv)
            return vrecip(rs[:, c0:c0 + n], rs[:, c0:c0 + n], t)

        def norm_rows(src, dst, junk, groups, *waits, c0=0, want=False, own=(None, None)):
            parts = [(src[:, t, a:b], junk[:, t, a:b], b - a, own[t]) for a, b in groups for t in range(2)]
            t_r = rstd(parts, *waits, c0=c0)
            toks = []
            for c, (a, b, t) in enumerate(((a, b, t) for a, b in groups for t in range(2)), c0):
                toks.append(vts(dst[:, t, a:b], src[:, t, a:b], rs[:, c:c + 1], None, ALU.mult, None, t_r))
            return (toks, t_r) if want else toks

        def prime(f):
            state["primed"] += 1
            act(sm[:, state["primed"]:state["primed"] + 1], onec, f, t_one)

        busy = [None, None]

        def splitter(order, first=1):
            todo, parts = list(order), {}

            def more():
                i = len(parts)
                if i == len(todo):
                    return
                n, b = todo[i], state["pair"]
                state["pair"] = 1 - b
                w = loads[n][0]
                m = w.shape[1]
                hi, lo = (W[:, b, j, 0:m * w.shape[2]].rearrange("p (a b) -> p a b", a=m) for j in range(2))
                a = act(hi, w, ACT.Copy, landed(n), busy[b])
                freed[n] = vtt(lo, w, hi.bitcast(F32), ALU.subtract, a)
                parts[n] = (hi, lo, freed[n], b)

            def done(n, tok):
                busy[parts[n][3]] = tok
                more()

            for _ in range(first):
                more()
            return parts, done, more

        def mm3(o, x, w, start, stop, waits, wide, sig=False):
            pairs = ((x[0], w[0]), (x[0], w[1]), (x[1], w[0])) if wide else ((w[0], x[0]), (w[0], x[1]), (w[1], x[0]))
            for i, (l, r) in enumerate(pairs):
                tok = mm(o, l, r, start and i == 0, stop and i == 2, waits if i == 0 else [], sig=sig and i == 2)
            return tok

        def to_parts(src, hi, lo, k0, nk, gain, waits, free):
            toks = []
            for k in range(0, nk, 2):
                b = nb()
                m = min(2, nk - k)
                for j in range(m):
                    for t in range(2):
                        last = tr(ps[:, b, j * T + t * P:j * T + (t + 1) * P],
                                  src[:, t, (k0 + k + j) * P:(k0 + k + j + 1) * P],
                                  waits, bank_free[b], sig=(j == m - 1 and t == 1))
                for j in range(m):
                    a = act(hi[:, k + j, :], ps[:, b, j * T:(j + 1) * T], ACT.Copy, last, t_cols, free, scale=gain(k + j))
                for j in range(m):
                    tk = vstt(lo[:, k + j, :], ps[:, b, j * T:(j + 1) * T], gain(k + j), hi[:, k + j, :].bitcast(F32),
                              ALU.mult, ALU.subtract, a)
                bank_free[b] = tk
                toks.append(tk)
            return toks

        def rows_parts(x, ks, where, ncols, waits, parts, done, before=(), width=512):
            nn = -(-ncols // width)
            bs = [[nb() for _ in range(nn)] for _ in range(2)]
            for i, k in enumerate(ks):
                s, kk = where(k)
                hi, lo, ready, _ = parts[s]
                for t in range(2):
                    for n in range(nn):
                        b = bs[t][n]
                        c = slice(n * width, min((n + 1) * width, ncols))
                        last = mm3(ps[:, b, 0:c.stop - c.start], [y[:, k, t * P:(t + 1) * P] for y in x],
                                   (hi[:, kk, c], lo[:, kk, c]), i == 0, i == len(ks) - 1,
                                   [waits(k), ready, bank_free[b] if i == 0 else None], True,
                                   sig=(t == 1 and n == nn - 1) or i == len(ks) - 1)
                if i + 1 < len(ks) and ks[i + 1] in before:
                    before[ks[i + 1]]()
                if i + 1 == len(ks) or where(ks[i + 1])[0] != s:
                    done(s, last)
            return bs, last

        def columns_parts(x, s, m, bank_ap, waits, parts):
            hi, lo, ready, _ = parts[s]
            c = slice(m * P, (m + 1) * P)
            for k in range(KD):
                tok = mm3(bank_ap, [y[:, k, :] for y in x], (hi[:, k, c], lo[:, k, c]), k == 0, k == KD - 1,
                          [waits, ready], False, sig=(k == KD - 1))
            return tok

        def to_columns(src, dst, k0, nk, gain, waits, free):
            toks = []
            for k in range(0, nk, 2):
                b = nb()
                m = min(2, nk - k)
                for j in range(m):
                    for t in range(2):
                        last = tr(ps[:, b, j * T + t * P:j * T + (t + 1) * P],
                                  src[:, t, (k0 + k + j) * P:(k0 + k + j + 1) * P],
                                  waits, bank_free[b], sig=(j == m - 1 and t == 1))
                if (k // 2) % 2 == 0:
                    for j in range(m):
                        tk = vts(dst[:, k + j, :], ps[:, b, j * T:(j + 1) * T], gain(k + j), None, ALU.mult, None,
                                 last, t_cols, free)
                else:
                    for j in range(m):
                        tk = act(dst[:, k + j, :], ps[:, b, j * T:(j + 1) * T], ACT.Copy, last, t_cols, free,
                                 scale=gain(k + j))
                bank_free[b] = tk
                toks.append(tk)
            return toks

        def rows_product(xT, nk, slots, per, ncols, waits):
            width = min(512, ncols)
            nn = -(-ncols // width)
            bs = [[nb() for _ in range(nn)] for _ in range(2)]
            last = None
            for k in range(nk):
                s = slots[k // per]
                w = slot(s, (per, ncols))
                for t in range(2):
                    for n in range(nn):
                        b = bs[t][n]
                        c1 = min((n + 1) * width, ncols)
                        end = k == nk - 1
                        free = k % per == per - 1 and t == 1 and n == nn - 1
                        tok = mm(ps[:, b, 0:c1 - n * width], xT[:, k, t * P:(t + 1) * P], w[:, k % per, n * width:c1],
                                 k == 0, end, waits, landed(s), bank_free[b] if k == 0 else None, sig=end or free)
                        if free or (end and t == 1 and n == nn - 1):
                            freed[s] = tok
                        last = tok or last
            return bs, last

        def columns_product(xT, slots, per, ncols, m, bank_ap, waits, sig):
            for k in range(KD):
                w = slot(slots[k // per], (per, ncols))
                tok = mm(bank_ap, w[:, k % per, m * P:(m + 1) * P], xT[:, k, :], k == 0, k == KD - 1,
                         waits, landed(slots[k // per]), sig=(k == KD - 1))
            return tok

        qrow = ar(0, 2, 768)
        krow = ar(1536, 2, 768)
        qT = ar(3072, 8, T)
        kT = ar(5120, 8, T)
        vm = ar(7168, 2, 512)
        qsT = ar(3072, 4, T)
        ksT = ar(4096, 4, T)
        vs = ar(8192, 2, 512)
        SM = ar(9216, 3072)
        Z = ar(12288, 3072)
        L = ar(15360, 3072)
        prow = SM[:, 0:1344].rearrange("p (t n) -> p t n", t=2)
        rp = SM[:, 1344:1344 + 2 * 8 * 16 * 2].rearrange("p (a t h d) -> p a t h d", a=2, t=2, h=8)
        rk = SM[:, 1856:1856 + 128].rearrange("p (a t d) -> p a t d", a=4, t=2)
        cs = SM[:, 1984:2048].rearrange("p (a t d) -> p a t d", a=2, t=2)
        ang = SM[:, 2048:2080].rearrange("p (t d) -> p t d", t=2)
        ak = SM[:, 2080:2112].rearrange("p (t d) -> p t d", t=2)
        posf = SM[:, 2112:2114]
        R8 = SM[0:8, 2560:3072]
        prime(ACT.Sqrt)
        t_u = norm_rows(h, u, u, [(0, D)], t_x)
        parts, done, ahead = splitter(L_a + L_qk + L_v + L_uq + [L_ukv])
        t_cols = stage_columns(3)
        t_uT = to_parts(u, *xin, 0, KD, lambda k: col("g_attn", k), t_u, None)
        ahead()

        bs = [[nb(), nb()] for _ in range(2)]
        for n, k0, m in [(s, k0, m) for s, (k0, m) in zip(L_a, ((0, 3), (3, 3), (6, 2)))]:
            hi, lo, ready, _ = parts[n]
            for k in range(k0, k0 + m):
                for t in range(2):
                    for c, (a, b_) in enumerate(((0, 384), (384, 672))):
                        last = mm3(ps[:, bs[t][c], 0:b_ - a], [y[:, k, t * P:(t + 1) * P] for y in xin],
                                   (hi[:, k - k0, a:b_], lo[:, k - k0, a:b_]), k == 0, k == KD - 1,
                                   [t_uT[k // 2], ready, bank_free[bs[t][c]] if k == 0 else None], True,
                                   sig=(t == 1 and c == 1))
            done(n, last)
        t_pr = []
        for t in range(2):
            bank_free[bs[t][0]] = act(prow[:, t, 0:384], ps[:, bs[t][0], 0:384], ACT.Copy, last)
            bank_free[bs[t][1]] = vcopy(prow[:, t, 384:672], ps[:, bs[t][1], 0:288], last)
            t_pr += [bank_free[bs[t][0]], bank_free[bs[t][1]]]

        def angles():
            t = vcopy(posf, posi[:, :], t_pos)
            ta = []
            for j in range(2):
                ta.append(vts(ang[:, j, :], invf, posf[:, j:j + 1], None, ALU.mult, None, t, t_inv))
            t = vts(ak, ang, 1.0 / TWO_PI, None, ALU.mult, None, ta)
            t = vts(ak, ak, MAGIC, None, ALU.add, None, t)
            t = vts(ak, ak, -MAGIC, None, ALU.add, None, t)
            for c in (C1, C2, C3):
                t = vstt(ang, ak, -c, ang, ALU.mult, ALU.add, t)
            t = vts(ang, ang, 3.1415925, -3.1415925, ALU.min, ALU.max, t)
            t_sin = act(cs[:, 1], ang, ACT.Sin, t)
            t = vts(ak, ang, -1.0, None, ALU.mult, None, t)
            t = vtt(ak, ak, ang, ALU.max, t)
            t = vts(ak, ak, -1.0, math.pi / 2, ALU.mult, ALU.add, t)
            t_cos = act(cs[:, 0], ak, ACT.Sin, t)
            return [t_sin, t_cos]

        t_qsk = []
        for i, s in enumerate(L_qk):
            dst = (qsT, ksT)[i // 2][:, 2 * (i % 2):2 * (i % 2) + 2, :]
            b = nb()
            for m in range(2):
                tk = columns_parts(xin, s, m, ps[:, b, m * T:(m + 1) * T], [t_uT, bank_free[b]], parts)
            done(s, tk)
            bank_free[b] = act(dst, ps[:, b, :].rearrange("p (a b) -> p a b", a=2), ACT.Copy, tk)
            t_qsk.append(bank_free[b])
            if i == 0:
                t_cs = angles()
            if i == 1:
                t_c = norm_rows(prow, prow, u[:, :, 0:640], [(0, 384), (384, 640)], t_pr, t_uT)

        def rope(x1, x2, o1, o2, c, s, tmp1, tmp2, *waits):
            a = vtt(tmp1, x2, s, ALU.mult, *waits)
            b_ = vtt(tmp2, x1, s, ALU.mult, *waits)
            c1 = vtt(o1, x1, c, ALU.mult, a, b_)
            c2 = vtt(o2, x2, c, ALU.mult, a, b_)
            d1 = vtt(o1, o1, tmp1, ALU.subtract, c1)
            d2 = vtt(o2, o2, tmp2, ALU.add, c2)
            return [d1, d2]

        t_kr = rope(prow[:, :, 640:656], prow[:, :, 656:672], prow[:, :, 640:656], prow[:, :, 656:672],
                    cs[:, 0], cs[:, 1], rk[:, 0], rk[:, 1], t_pr, t_cs)

        SBS = 64 ** -0.5
        MLS = 96 ** -0.5

        def halves(buf):
            return (buf[:, 0:1024].rearrange("p (h k) -> p h k", h=8),
                    buf[:, 1024:3072].rearrange("p (h k) -> p h k", h=8))

        def pair_scores(qx, kx, waits):
            b0 = [nb(), nb()]
            for i in range(4):
                for par in range(2):
                    pp = slice(64 * par, 64 * par + 64)
                    last = mm(ps[:, b0[par], i * P:(i + 1) * P], qx[pp, i, 0:P], kx[pp, i, 0:P], True, True, waits,
                              bank_free[b0[par]], sig=(i == 3))
            b1 = [[nb(), nb()], [nb(), nb()]]
            for i in range(4):
                for par in range(2):
                    pp = slice(64 * par, 64 * par + 64)
                    b = b1[par][i // 2]
                    last = mm(ps[:, b, (i % 2) * T:(i % 2) * T + T], qx[pp, i, P:T], kx[pp, i, :], True, True, waits,
                              bank_free[b], sig=(i == 3))
            return b0, b1, last

        for tile in (0, 1, 2):
            t_cols = [t_cols, stage_columns(tile)]
        b0, b1, last = pair_scores(qsT, ksT, t_qsk)
        Z0, Z1 = halves(Z)
        L0, L1 = halves(L)
        t_z = [[], []]
        for par in range(2):
            bank_free[b0[par]] = vstt(Z0[:, 4 * par:4 * par + 4, :], ps[:, b0[par], :].rearrange("p (a b) -> p a b", a=4),
                                      SBS, bc(msk[:, 1, P:T].unsqueeze(1), [P, 4, P]), ALU.mult, ALU.add, last, t_msk, t_cols)
            t_z[0].append(bank_free[b0[par]])
        for par in range(2):
            for i in range(2):
                b = b1[par][i]
                bank_free[b] = vstt(Z1[:, 4 * par + 2 * i:4 * par + 2 * i + 2, :],
                                    ps[:, b, :].rearrange("p (a b) -> p a b", a=2), SBS,
                                    bc(msk[:, 1, :].unsqueeze(1), [P, 2, T]), ALU.mult, ALU.add, last, t_msk, t_cols)
                t_z[1].append(bank_free[b])
        zl = [(Z[:, 0:1024], L[:, 0:1024], L0, P), (Z[:, 1024:3072], L[:, 1024:3072], L1, T)]
        t = [act(l_, z, ACT.Abs, t_z[i]) for i, (z, l_, _, _) in enumerate(zl)]
        t = [act(l_, l_, ACT.Exp, t[i], scale=-1.0) for i, (_, l_, _, _) in enumerate(zl)]
        t = [act(l_, l_, ACT.Ln, t[i], bias=1.0) for i, (_, l_, _, _) in enumerate(zl)]
        t_sum = []

        def stick_sums(i):
            z, l_, lh, n = zl[i]
            a = vstt(l_, z, 0.0, l_, ALU.max, ALU.add, t[i])
            sc = []
            for hd in range(8):
                r = lh[:, hd, ::-1]
                sc.append(V(lambda e, r=r, n=n: e.tensor_tensor_scan(r, bc(onec, [P, n]), r, 0.0, ALU.mult, ALU.subtract),
                            a, t_one))
            t_sum.append(vtt(l_, l_, z, ALU.add, sc))

        rb = nb()
        t_rb = mm(ps[0:8, rb, :], rel, oht, True, True, t_rel, t_oht, bank_free[rb], sig=True)
        stick_sums(0)
        bs, last = rows_parts(xin, range(KD), lambda k: (L_v[k // 4], k % 4), 512, lambda k: t_uT, parts,
                              lambda n, tok: done(n, tok) if n == L_v[0] else None)
        t_in = last
        t_cT = to_parts(prow, *xin, 0, 5, lambda k: col("g_cq", k) if k < 3 else col("g_ckv", k - 3), t_c, t_in)
        done(L_v[1], last)
        stick_sums(1)
        t_vs = []
        for t in range(2):
            bank_free[bs[t][0]] = act(vs[:, t, :], ps[:, bs[t][0], :], ACT.Copy, last)
            t_vs.append(bank_free[bs[t][0]])
        bank_free[rb] = act(R8, ps[0:8, rb, :], ACT.Copy, t_rb)
        t_skew = dma(G, "d_skew", skew, bc(R8.unsqueeze(1), [8, P, 512]), bank_free[rb])

        t_w = [act(zl[0][1], zl[0][1], ACT.Exp, t_sum[0])]
        bs, last = rows_parts(xin, (0, 1, 2), lambda k: (L_uq[k // 2], k % 2), 768, lambda k: t_cT[k // 2], parts, done,
                              width=384)
        t_q = []
        for t in range(2):
            for c in range(2):
                b = bs[t][c]
                bank_free[b] = act(qrow[:, t, c * 384:(c + 1) * 384], ps[:, b, 0:384], ACT.Copy, last)
                t_q.append(bank_free[b])
        t_w.append(act(zl[1][1], zl[1][1], ACT.Exp, t_sum[1]))
        bs, last = rows_parts(xin, (3, 4), lambda k: (L_ukv, k - 3), 1024, lambda k: t_cT[k // 2], parts, done)
        kh = krow.rearrange("p t (h d) -> p t h d", h=8)
        qh = qrow.rearrange("p t (h d) -> p t h d", h=8)
        vh = vm.rearrange("p t (h d) -> p t h d", h=8)
        t_qr = []
        for t in range(2):
            cb = bc(cs[:, 0, t].unsqueeze(1), [P, 8, 16])
            sb_ = bc(cs[:, 1, t].unsqueeze(1), [P, 8, 16])
            t_qr += rope(qh[:, t, :, 64:80], qh[:, t, :, 80:96], qh[:, t, :, 64:80], qh[:, t, :, 80:96],
                         cb, sb_, rp[:, 0, t], rp[:, 1, t], t_q, t_cs)
        t_k, t_vm = [], []
        for t in range(2):
            t_k.append(vcopy(kh[:, t, :, 64:96], bc(prow[:, t, 640:672].unsqueeze(1), [P, 8, 32]), t_kr, t_in))
            for c in range(2):
                b = bs[t][c]
                src = ps[:, b, :].rearrange("p (h d) -> p h d", h=4)
                t_k.append(vcopy(kh[:, t, 4 * c:4 * c + 4, 0:64], src[:, :, 0:64], last))
                bank_free[b] = act(vh[:, t, 4 * c:4 * c + 4, :], src[:, :, 64:128], ACT.Copy, t_k[-1])
                t_vm.append(bank_free[b])

        def heads_to_columns(src, dst, waits):
            toks = []
            for hd in range(0, 8, 2):
                b = nb()
                for j in range(2):
                    for t in range(2):
                        last = tr(ps[0:96, b, j * T + t * P:j * T + (t + 1) * P],
                                  src[:, t, (hd + j) * 96:(hd + j + 1) * 96], waits, bank_free[b],
                                  sig=(j == 1 and t == 1))
                o, i = dst[0:96, hd:hd + 2, :], ps[0:96, b, :].rearrange("p (a b) -> p a b", a=2)
                bank_free[b] = act(o, i, ACT.Copy, last) if hd % 4 else vcopy(o, i, last)
                toks.append(bank_free[b])
            return toks

        t_qT = heads_to_columns(qrow, qT, t_qr)
        t_kT = heads_to_columns(krow, kT, t_k)

        bm0 = [nb(), nb()]
        for hd in range(8):
            b = bm0[hd // 4]
            last0 = mm(ps[:, b, (hd % 4) * P:(hd % 4 + 1) * P], qT[0:96, hd, 0:P], kT[0:96, hd, 0:P], True, True,
                       t_qT[hd // 2], t_kT[hd // 2], bank_free[b], sig=(hd % 4 == 3))
        bm1 = [nb() for _ in range(4)]
        t_m1 = []
        for hd in range(8):
            b = bm1[hd // 2]
            last1 = mm(ps[:, b, (hd % 2) * T:(hd % 2 + 1) * T], qT[0:96, hd, P:T], kT[0:96, hd, :], True, True,
                       bank_free[b], sig=(hd % 2 == 1))
            t_m1.append(last1)
        S0, S1 = halves(SM)
        t_s0, t_s1 = [], []
        sm_free = [t_qr, t_k, t_cT, t_skew]
        for j in range(2):
            bank_free[bm0[j]] = vstt(S0[:, 4 * j:4 * j + 4, :], ps[:, bm0[j], :].rearrange("p (a b) -> p a b", a=4), MLS,
                                     bc(msk[:, 0, P:T].unsqueeze(1), [P, 4, P]), ALU.mult, ALU.add, last0, t_msk, sm_free)
            t_s0.append(bank_free[bm0[j]])
        for j in range(4):
            bank_free[bm1[j]] = vstt(S1[:, 2 * j:2 * j + 2, :], ps[:, bm1[j], :].rearrange("p (a b) -> p a b", a=2), MLS,
                                     bc(msk[:, 0, :].unsqueeze(1), [P, 2, T]), ALU.mult, ALU.add, t_m1[2 * j + 1], t_msk, sm_free)
            t_s1.append(bank_free[bm1[j]])

        mx = sm[:, 120:136]
        rsum = sm[:, 136:152]

        def softmax(buf, w0, w1, both):
            s0, s1 = halves(buf)
            d = []
            for t, (st, w) in enumerate(((s0, w0), (s1, w1))):
                m = mx[:, 8 * t:8 * t + 8]
                a = vred(m, st, ALU.max, w)
                if t and both:
                    d.append(vtt(st, st, bc(m.unsqueeze(2), [P, 8, T]), ALU.subtract, a))
                else:
                    d.append(vts(m, m, -1.0, None, ALU.mult, None, a))
            x = []
            for c in range(8 if both else 16):
                st = (s0, s1)[c // 8][:, c % 8, :]
                x.append(act(st, st, ACT.Exp, d[c // 8], bias=mx[:, c:c + 1], accum_out=rsum[:, c:c + 1]))
            if both:
                x += [act(s1, s1, ACT.Exp, d[1])] * 8
            return x, x[-1]

        def softmax_sums(buf, x1, both):
            if both:
                x1 = vred(rsum[:, 8:16], halves(buf)[1], ALU.add, x1)
            return vrecip(rsum, rsum, x1)

        def weigh_columns(buf, order, PT, waits, ptfree, engines):
            s0, s1 = halves(buf)
            blocks = [(order(hd), s0[:, order(hd), :]) for hd in range(8)]
            for hd in range(8):
                blocks += [(8 + order(hd), s1[:, order(hd), 0:P]), (8 + order(hd), s1[:, order(hd), P:T])]
            toks = [None] * 24
            for g in range(0, 24, 4):
                b = nb()
                for j in range(4):
                    last = tr(ps[:, b, j * P:(j + 1) * P], blocks[g + j][1], waits(blocks[g + j][0]), bank_free[b], sig=(j == 3))
                o = PT[:, g * P:(g + 4) * P]
                if engines[(g // 4) % len(engines)] is A:
                    bank_free[b] = act(o, ps[:, b, :], ACT.Copy, last, ptfree)
                else:
                    bank_free[b] = vcopy(o, ps[:, b, :], last, ptfree)
                for j in range(4):
                    toks[g + j] = bank_free[b]
            return toks, last

        def weigh_values(PT, v, toks, vwaits):
            bo = [nb(), nb()]
            pt = PT.rearrange("p (a q) -> p a q", q=P)
            vv = v.rearrange("p t (h d) -> p t h d", h=8)
            for hd in range(8):
                t0 = mm(ps[:, bo[0], hd * 64:hd * 64 + 64], pt[:, hd, :], vv[:, 0, hd, :], True, True,
                        toks[hd], bank_free[bo[0]], vwaits, sig=(hd == 7))
            for hd in range(8):
                o = ps[:, bo[1], hd * 64:hd * 64 + 64]
                mm(o, pt[:, 8 + 2 * hd, :], vv[:, 0, hd, :], True, False, toks[8 + 2 * hd], bank_free[bo[1]])
                t1 = mm(o, pt[:, 9 + 2 * hd, :], vv[:, 1, hd, :], False, True, sig=(hd == 7))
            return bo, (t0, t1)

        mixed = u
        parity = lambda hd: 4 * (hd % 2) + hd // 2
        tk, t_lfree = weigh_columns(L, parity, Z, lambda i: t_w[i // 8], t_sum, [A])
        bo, t_sv = weigh_values(Z, vs, tk, t_vs)
        t_e, t_r = softmax(SM, t_s0, t_s1, False)
        t_m = []
        for t in range(2):
            bank_free[bo[t]] = vcopy(mixed[:, t, 512:1024], ps[:, bo[t], :], t_sv[t], t_in)
            t_m.append(bank_free[bo[t]])
        t_r = softmax_sums(SM, t_r, False)
        junk = ar(8192, 2, 512)
        sbh, mlh = mixed[:, :, 512:1024], mixed[:, :, 0:512]
        PT = ar(3072, 3072)
        tk, _ = weigh_columns(SM, lambda hd: hd, PT, lambda i: t_e[i], last1, [V, A])
        t_sn = norm_rows(sbh, sbh, junk, [(0, 512)], t_m, c0=2)
        arena_free = [t_w, t_lfree, t_sv[1]]
        parts, done, ahead = splitter([L_o[j] for j in (2, 3, 0, 1)])
        bo, t_mv = weigh_values(PT, vm, tk, t_vm)
        t_ms = to_parts(sbh, X[:, 0, 4:8], X[:, 1, 4:8], 0, 4, lambda k: col("g_out_sb", k), t_sn, None)
        ahead()
        t_m = []
        for t in range(2):
            o = mlh[:, t].rearrange("p (h d) -> p h d", h=8)
            i = ps[:, bo[t], :].rearrange("p (h d) -> p h d", h=8)
            bank_free[bo[t]] = vtt(o, i, bc(rsum[:, 8 * t:8 * t + 8].unsqueeze(2), [P, 8, 64]), ALU.mult, t_mv[t], t_r)
            t_m.append(bank_free[bo[t]])
        t_mn = norm_rows(mlh, mlh, junk, [(0, 512)], t_m)
        t_mm = []

        def latent_half():
            t_mm.extend(to_parts(mlh, *xin, 0, 4, lambda k: col("g_out_mla", k), t_mn, None))

        bs, last = rows_parts(xin, (4, 5, 6, 7, 0, 1, 2, 3), lambda k: (L_o[k // 2], k % 2), 1024,
                              lambda k: t_ms[k // 2 - 2] if k >= 4 else t_mm[k // 2], parts, done, {0: latent_half})
        t_h = []
        for t in range(2):
            for n in range(2):
                b = bs[t][n]
                hs = h[:, t, n * 512:(n + 1) * 512]
                bank_free[b] = vtt(hs, hs, ps[:, b, :], ALU.add, last)
                t_h.append(bank_free[b])
        t_mT = t_mm

        def finish(waits, src=h):
            waits = flat(waits)
            o = out[0].rearrange("(t p) d -> p t d", p=P)
            if len(waits) != 4:
                return [dma(SP, "d_out", o, src[:, :, :], waits)]
            return [dma(SP, f"d_out{t}", o[:, t, :], src[:, t, :], waits[2 * t:2 * t + 2]) for t in range(2)]

        def run(done):
            q = Queue(SP.sem)
            q.items = list(SP.items[:NX])
            for n, (dst, src, i, before, _) in enumerate(loads):
                if n == L_pp and stop != "attn":
                    q.raw(lambda e: most.__setitem__(q, e.value_load(over, min_val=0, max_val=T - 1)), t_over)
                    rounds(q, OD)
                if before is not None and before not in freed:
                    break
                w = [freed[before]] if before is not None else [arena_free if i >= NSLOT else None]
                q(lambda e, d=dst, s_=src, sm_=slot_sem[i]: e.dma_start(d, s_).then_inc(sm_, 16), w, sig=False)
            q.items += SP.items[NX:]
            SP.items = q.items
            SP.items.append((done[:-1], lambda e: e.wait_ge(*done[-1]), False))
            block = ctx.enter_context(nc.Block())

            @block.sync
            def _(e):
                SP.emit(e)

            @block.gpsimd
            def _(e):
                G.emit(e)

            @block.scalar
            def _(e):
                A.emit(e)

            @block.vector
            def _(e):
                V.emit(e)

            @block.tensor
            def _(e):
                PE.emit(e)

        if stop == "attn":
            return run(finish([t_h, t_wr, t_brt]))

        posm = sm[:, 160:224].rearrange("p (t e) -> p t e", t=2)
        gate = sm[:, 224:288].rearrange("p (t e) -> p t e", t=2)
        t_sb = [PE.last(), V.last(), A.last()]
        Sr = X[:, :, :, :].rearrange("p a k t -> p (a k t)").rearrange("p (t e s) -> p t e s", t=2, e=NE)
        GTr = W[:, :, :, :].rearrange("p a b n -> p (a b n)").rearrange("p (e t) -> p e t", e=NE)
        S, GT = Sr.bitcast(F32), GTr.bitcast(F32)
        bgu = ar(0, 2048)
        xg = [ar(2048 + 2048 * i, KD, 4 * CAP) for i in range(2)]
        glu, lin, sig, actv = (ar(6144 + 512 * i, 512) for i in range(4))
        uTp = ar(8192, KD, T)
        actT = [ar(8192 + 512 * i, 4, P) for i in range(2)]
        yb = [ar(9216 + 512 * i, 512) for i in range(2)]
        lg = ar(10240, 2, NE)
        v8 = ar(10304, 2, 8)
        i8 = ar(10320, 2, 8).bitcast(U32)
        f8 = ar(10336, 2, 8)
        e8 = ar(10352, 2, 4)
        z8 = ar(10360, 2)
        i32 = ar(10368, NE)
        tri = ar(10400, P)
        mk = ar(10528, 2, NE)
        oh = ar(10592, 2, 4, NE)
        gT = ar(10848, T)
        gs = ar(11104, NE)
        bdn = ar(11136, D)
        stk = ar(12160, NE)
        lgq = gT
        Sg = msk[:, 0:2, :].rearrange("p t (e c s) -> p t e c s", e=2, c=2)

        t0 = G(lambda e: e.memset(tri, 1.0), t_sb)
        t_tri = G(lambda e: e.affine_select(out=tri, in_=tri, compare_op=ALU.is_ge, fill=0.0, base=0,
                                            pattern=[[1, P]], channel_multiplier=-1), t0)
        t_i32 = G(lambda e: e.iota(i32, [[1, NE]], base=0, channel_multiplier=0, allow_small_or_imprecise_dtypes=True))
        a = G(lambda e: e.memset(stk, 0.0))
        for q in range(4):
            a = t_stk = G(lambda e, q=q: e.affine_select(out=stk, in_=stk, compare_op=ALU.not_equal, fill=1.0, base=-32 * q,
                                                         pattern=[[-1, NE]], channel_multiplier=1), a)
        t_bz = G(lambda e: e.memset(bgu, 0.0))
        t_bgu = dma(G, "d_bgu", bgu[0:NE, :], I["b_gu"][0], t_bz)
        t_bdn = dma(G, "d_bdn", bdn[0:NE, :], I["b_dn"][0])

        t_u, t_r = norm_rows(h, u, u, [(0, D)], t_h, t_mT, want=True)
        prime(ACT.Exp)
        t_uT = to_columns(h, uTp, 0, KD, lambda k: col("g_moe", k), t_h, t_sb)
        b = nb()
        for k in range(KD):
            q = slice(32 * (k % 4), 32 * (k % 4) + 32)
            last = mm(ps[q, b, 0:T], wr[:, k, :], uTp[:, k, :], k < 4, k >= 4, t_uT[k // 2], t_wr, bank_free[b], sig=(k == KD - 1))
        a = bank_free[b] = act(lgq, ps[:, b, 0:T], ACT.Copy, last, t_sb)
        bl = [nb(), nb()]
        for t in range(2):
            last = mm(ps[:, bl[t], 0:NE], lgq[:, t * P:(t + 1) * P], stk, True, True, a, t_stk, bank_free[bl[t]], sig=(t == 1))
        t_m8 = []
        for t in range(2):
            a = bank_free[bl[t]] = vstt(lg[:, t, :], ps[:, bl[t], 0:NE], rs[:, t:t + 1], brt, ALU.mult, ALU.add, last, t_r, t_brt, t_sb)
            a = V(lambda e, t=t: e.max(v8[:, t, :], lg[:, t, :]), a)
            t_m8.append(V(lambda e, t=t: e.max_index(i8[:, t, :], v8[:, t, :], lg[:, t, :]), a))
        a = vtt(e8, v8[:, :, 0:4], bc(v8[:, :, 0:1], [P, 2, 4]), ALU.subtract, t_m8)
        x = act(e8, e8, ACT.Exp, a)
        a = vcopy(f8, i8, t_m8)
        o = vtt(oh, bc(i32.unsqueeze(1).unsqueeze(1), [P, 2, 4, NE]), bc(f8[:, :, 0:4].unsqueeze(3), [P, 2, 4, NE]),
                ALU.is_equal, a, t_i32, t_sb)
        a = vred(z8, e8, ALU.add, x)
        a = vrecip(z8, z8, a)
        a = vtt(e8, e8, bc(z8.unsqueeze(2), [P, 2, 4]), ALU.mult, a)
        a = vtt(oh, oh, bc(e8.unsqueeze(3), [P, 2, 4, NE]), ALU.mult, a, o)
        t_g = vred(gate, oh.rearrange("p t j e -> p t e j"), ALU.add, a)
        t_mk = vts(mk, gate, 0.0, None, ALU.is_gt, None, t_g)
        b = nb()
        mm(ps[:, b, 0:NE], tri, mk[:, 0, :], True, True, t_mk, t_tri, bank_free[b])
        mm(ps[:, b, NE:2 * NE], bc(onec, [P, P]), mk[:, 0, :], True, False)
        last = mm(ps[:, b, NE:2 * NE], tri, mk[:, 1, :], False, True, sig=True)
        t = vtt(posm, ps[:, b, 0:2 * NE].rearrange("p (t e) -> p t e", t=2), mk, ALU.mult, last)
        bank_free[b] = t
        t_pm = vts(posm, posm, -1.0, None, ALU.add, None, t)
        t_S = []
        for j in range(8):
            c = slice(4 * j, 4 * j + 4)
            t_S.append(vtt(Sr[:, :, c, :], bc(iota.unsqueeze(1).unsqueeze(1), [P, 2, 4, CAP]),
                           bc(posm[:, :, c].unsqueeze(3), [P, 2, 4, CAP]), ALU.is_equal, t_pm, t_iota, t_sb))

        Y = [[0, 1], [2, 3]]
        GB, LB, DB, TB = 4, 5, 6, 7
        t_xg = {}
        gu_tok = {}

        def gather(j, i, bank):
            dst = xg[j % 2]
            for a in range(2):
                k = 2 * i + a
                for t in range(2):
                    last = mm(ps[:, bank, a * 256:(a + 1) * 256], u[:, t, k * P:(k + 1) * P], S[:, t, 4 * j:4 * j + 4, :],
                              t == 0, t == 1, t_S[j], bank_free[bank], sig=(t == 1 and a == 1))
            for a in range(2):
                k = 2 * i + a
                bank_free[bank] = act(dst[:, k, :], ps[:, bank, a * 256:(a + 1) * 256], ACT.Copy, last,
                                      [gu_tok[4 * j - 5]] if j >= 2 else None, scale=col("g_moe", k))
            t_xg.setdefault(j, []).append(bank_free[bank])

        def first_sums():
            for t in range(2):
                a = tr(ps[0:NE, TB, t * P:(t + 1) * P], gate[:, t, :], t_g, bank_free[TB], sig=True)
            a = bank_free[TB] = vcopy(gT[0:NE, :], ps[0:NE, TB, 0:T], a)
            for t in range(2):
                for c in range(2):
                    a = mm(ps[:, Y[t][c], :], gT[0:NE, t * P:(t + 1) * P], bdn[0:NE, c * 512:(c + 1) * 512], True, False,
                           a, t_bdn, bank_free[Y[t][c]], sig=(t == 1 and c == 1)) or a

        over = posi[0:1, 0:1]
        m1 = sm[:, 296:297]
        most = {}

        def longest():
            a = vred(m1, sm[:, 160:224], ALU.max, t_pm)
            a = tr(ps[0:1, TB, 0:P], m1, a, bank_free[TB], sig=True)
            a = bank_free[TB] = vred(sm[0:1, 297:298], ps[0:1, TB, 0:P], ALU.max, a)
            a = vcopy(over, sm[0:1, 297:298], a, t_pos)
            for q in (PE, A, V):
                q.raw(lambda e, q=q: most.__setitem__(q, e.value_load(over, min_val=0, max_val=T - 1)), a)
            return a

        t_GT, t_gs = [], []

        def place_columns(i):
            c = slice(2 * i, 2 * i + 2)
            ts = [vcopy(Sg[:, t], bc(S[:, t, c, :].unsqueeze(2), [P, 2, 2, CAP]), t_S[i // 2], state.get("sg"), t_sb)
                  for t in range(2)]
            for j in range(2):
                for t in range(2):
                    a = tr(ps[:, TB, j * T + t * P:j * T + (t + 1) * P], Sg[:, t, j].rearrange("p c s -> p (c s)"), ts,
                           bank_free[TB], sig=(j == 1 and t == 1))
            state["sg"] = a
            for j in range(2):
                for t in range(2):
                    g = mm(ps[:, DB, j:j + 1], Sg[:, t, j].rearrange("p c s -> p (c s)"), gate[:, t, 2 * i + j:2 * i + j + 1],
                           t == 0, t == 1, t_g, bank_free[DB], sig=(j == 1 and t == 1))
            state["sg"] = g
            bank_free[DB] = vcopy(gs[:, c], ps[:, DB, 0:2], g)
            t_gs.append(bank_free[DB])
            bank_free[TB] = act(GTr[:, c, :], ps[:, TB, :].rearrange("p (a b) -> p a b", a=2), ACT.Copy, a, t_sb)
            t_GT.append(bank_free[TB])

        t_act, t_aT, t_yb, t_dn, t_sc2 = {}, {}, {}, {}, {}

        def experts_up(e):
            x = xg[(e // 4) % 2]
            c0 = (e % 4) * CAP
            if e:
                experts_bias(e)
            for k in range(KD):
                if e == 0 and k % 2 == 0 and k < 6:
                    gather(0, k // 2 + 1, k // 2 + 1)
                w = slot(L_gu[e][k])
                for half, bank in ((0, GB), (1, LB)):
                    for c in range(2):
                        tok = mm(ps[c * 64:c * 64 + 64, bank, :], x[:, k, c0:c0 + CAP],
                                 w[:, half * D + c * 512:half * D + (c + 1) * 512], False, k == KD - 1,
                                 t_xg[e // 4] if e else t_xg[0][k // 2], landed(L_gu[e][k]), sig=(half == 1 and c == 1))
                freed[L_gu[e][k]] = tok
            gu_tok[e] = tok

        def experts_bias(e):
            for half, bank in ((0, GB), (1, LB)):
                for c in range(2):
                    mm(ps[c * 64:c * 64 + 64, bank, :], bc(ident[:, e:e + 1], [P, CAP]),
                       bgu[:, half * D + c * 512:half * D + (c + 1) * 512], True, False, t_bgu, bank_free[bank])

        def experts_act(e):
            tok = gu_tok[e]
            tg = vts(glu, ps[:, GB, :], 7.0, None, ALU.min, None, tok, t_act.get(e - 1))
            bank_free[GB] = tg
            t_sg = act(sig, glu, ACT.Sigmoid, tg, scale=1.702)
            tl = vts(lin, ps[:, LB, :], 7.0, -7.0, ALU.min, ALU.max, tok, t_act.get(e - 1))
            bank_free[LB] = tl
            ta = vstt(lin, lin, 1.0, glu, ALU.add, ALU.mult, tl, tg)
            t_act[e] = vtt(actv, lin, sig, ALU.mult, ta, t_sg, t_aT.get(e - 1))

        def experts_turn(e):
            for j in range(4):
                last = tr(ps[:, TB, j * P:(j + 1) * P], actv[:, j * P:(j + 1) * P], t_act[e], bank_free[TB], sig=(j == 3))
            t_aT[e] = bank_free[TB] = act(actT[e % 2], ps[:, TB, :].rearrange("p (j m) -> p j m", j=4), ACT.Copy, last,
                                          t_dn.get(e - 2))

        def experts_down(e):
            for kk in range(KD):
                w = slot(L_dn[e][kk // 2], (2, D))
                a = actT[e % 2][:, kk % 4, (kk // 4) * 64:(kk // 4) * 64 + 64]
                for c in range(2):
                    tok = mm(ps[c * 64:c * 64 + 64, DB, :], a, w[:, kk % 2, c * 512:(c + 1) * 512], kk == 0, kk == KD - 1,
                             t_aT[e], landed(L_dn[e][kk // 2]), bank_free[DB], sig=(c == 1 and kk % 2 == 1))
                if kk % 2:
                    freed[L_dn[e][kk // 2]] = tok
            t_dn[e] = tok
            t_yb[e] = bank_free[DB] = act(yb[e % 2], ps[:, DB, :], ACT.Copy, tok, t_sc2.get(e - 2), t_gs[e // 2],
                                          scale=gs[:, e:e + 1])

        def experts_scatter(e):
            for t in range(2):
                for c in range(2):
                    tok = mm(ps[:, Y[t][c], :], GT[c * 64:c * 64 + 64, e, t * P:(t + 1) * P], yb[e % 2][c * 64:c * 64 + 64, :],
                             False, e == NE - 1, t_yb[e], t_GT[e // 2], sig=(t == 1 and c == 1))
            t_sc2[e] = tok

        experts_bias(0)
        gather(0, 0, 0)
        lam0, lam1 = sm[:, 288:292], sm[:, 292:296]

        def decay():
            lam = cols[:, col0[0] + rows["lam_2"][1]:col0[0] + rows["lam_2"][1] + 4]
            a = act(lam0, lam, ACT.Abs, t_cols)
            a = act(lam0, lam0, ACT.Exp, a, scale=-1.0)
            a = act(lam0, lam0, ACT.Ln, a, bias=1.0)
            b_ = vts(lam1, lam, -1.0, 0.0, ALU.mult, ALU.max, t_cols)
            a = vtt(lam0, lam0, lam1, ALU.add, a, b_)
            return vts(lam0, lam0, -8.0, None, ALU.mult, None, a)

        for e in range(NE):
            experts_up(e)
            if e == 1:
                experts_turn(0)
            experts_act(e)
            if e == 0:
                continue
            if e == 1 or e % 2 == 0:
                place_columns(e // 2)
            experts_down(e - 1)
            if e == 1:
                first_sums()
                experts_turn(1)
                gather(1, 0, TB)
                continue
            if e == 2:
                t_over = longest()
                gather(1, 1, TB)
                experts_turn(2)
                experts_scatter(0)
                experts_scatter(1)
                t_lam = decay()
                continue
            if e == 3:
                gather(1, 2, TB)
            if e < NE - 4:
                gather(e // 4 + 1, e % 4, TB)
            experts_turn(e)
            experts_scatter(e - 1)
        experts_down(NE - 1)
        experts_scatter(NE - 1)
        t_h = []
        for t in range(2):
            for c in range(2):
                hs = h[:, t, c * 512:(c + 1) * 512]
                bank_free[Y[t][c]] = vtt(hs, hs, ps[:, Y[t][c], :], ALU.add, t_sc2[NE - 1])
                t_h.append(bank_free[Y[t][c]])

        OP, OA, OV, OD = (Round(sem(f"s_o{n}")) for n in "pavd")
        MORE = T // CAP - 1
        bgo = ar(0, 2048)
        xo = ar(2048, KD, CAP)
        GTo = ar(2560, T)
        So = ar(2816, 2, CAP)
        Sgo = ar(2944, 2, 2 * CAP)
        tb, gt, tt = (ar(3200 + 2 * MORE * NE * i, 2, MORE * NE) for i in range(3))
        wgu_o = ring[:, :, :]
        wdn_o = ar(10240, KD, D)
        loop_deps = [t_sc2[NE - 1], t_h]
        s_set = sem("s_set")
        s_end = sem("s_end")

        def prepare(e):
            ins = [e.memset(bgo, 0.0)]
            for r in range(MORE):
                ins.append(e.tensor_scalar(tb[:, :, r * NE:(r + 1) * NE], posm, -float(CAP * (r + 1)), None, ALU.add))
                ins.append(e.tensor_copy(gt[:, :, r * NE:(r + 1) * NE], gate))
            for x in ins:
                x.then_inc(s_set, 1)
            e.wait_ge(s_set, len(ins))

        o_dma = [OD(lambda e, i: e.dma_start(wgu_o, I["w_gu"][0, bass.ds(i % NE, 1), :, :].rearrange(
                     "a (k p) n -> p (a k) n", p=P)), sig=16),
                 OD(lambda e, i: e.dma_start(wdn_o, I["w_dn"][0, bass.ds(i % NE, 1), :, :].rearrange(
                     "a (k p) n -> p (a k) n", p=P)), sig=16),
                 OD(lambda e, i: e.dma_start(bgo[0:1, :], I["b_gu"][0, bass.ds(i % NE, 1), :]), sig=16)][-1]
        oS = []
        for t in range(2):
            a = OV(lambda e, i, t=t: e.tensor_scalar(So[:, t, :], iota, tb[:, t, 0:1], None, ALU.is_equal), o_dma)
            oS.append(a)
            for c in range(2):
                oS.append(OV(lambda e, i, t=t, c=c: e.tensor_scalar(Sgo[:, t, c * CAP:(c + 1) * CAP], So[:, t, :],
                                                                    gt[:, t, 0:1], None, ALU.mult), a))
        for x in (tb, gt):
            a = OV(lambda e, i, x=x: e.tensor_copy(tt[:, :, 0:MORE * NE - 1], x[:, :, 1:MORE * NE]), oS)
            oS = [OV(lambda e, i, x=x: e.tensor_copy(x[:, :, 0:MORE * NE - 1], tt[:, :, 0:MORE * NE - 1]), a)]

        def omm(o, l, r, start, stop, *waits, sig=0):
            return OP(lambda e, i: e.matmul(o, l, r, start=start, stop=stop), *waits, sig=sig)

        for k in range(KD):
            for t in range(2):
                a = omm(ps[:, GB, k * CAP:(k + 1) * CAP], u[:, t, k * P:(k + 1) * P], So[:, t, :], t == 0, t == 1, oS,
                        sig=int(k == KD - 1 and t == 1))
        ox = [OA(lambda e, i, k=k: e.activation(xo[:, k, :], ps[:, GB, k * CAP:(k + 1) * CAP], ACT.Copy,
                                                scale=col("g_moe", k)), a) for k in range(KD)]
        for t in range(2):
            a = OP(lambda e, i, t=t: e.transpose(ps[:, DB, t * P:(t + 1) * P], Sgo[:, t, :], ident[:, :]), oS, sig=t)
        oG = OA(lambda e, i: e.activation(GTo, ps[:, DB, 0:T], ACT.Copy), a)
        for half, bank in ((0, GB), (1, LB)):
            for c in range(2):
                w0 = half * D + c * 512
                omm(ps[c * 64:c * 64 + 64, bank, :], bc(ident[:, 0:1], [P, CAP]), bgo[:, w0:w0 + 512], True, False, ox, o_dma)
                for k in range(KD):
                    a = omm(ps[c * 64:c * 64 + 64, bank, :], xo[:, k, :], wgu_o[:, k, w0:w0 + 512], False, k == KD - 1,
                            sig=int(half == 1 and c == 1 and k == KD - 1))
        g = OV(lambda e, i: e.tensor_scalar(glu, ps[:, GB, :], 7.0, None, ALU.min), a)
        sg = OA(lambda e, i: e.activation(sig, glu, ACT.Sigmoid, scale=1.702), g)
        a = OV(lambda e, i: e.tensor_scalar(lin, ps[:, LB, :], 7.0, -7.0, ALU.min, ALU.max), a)
        a = OV(lambda e, i: e.scalar_tensor_tensor(out=lin, in0=lin, scalar=1.0, in1=glu, op0=ALU.add, op1=ALU.mult), a, g)
        a = OV(lambda e, i: e.tensor_tensor(actv, lin, sig, ALU.mult), a, sg)
        for j in range(4):
            a = OP(lambda e, i, j=j: e.transpose(ps[:, TB, j * P:(j + 1) * P], actv[:, j * P:(j + 1) * P], ident[:, :]), a,
                   sig=int(j == 3)) if j == 0 else OP(
                       lambda e, i, j=j: e.transpose(ps[:, TB, j * P:(j + 1) * P], actv[:, j * P:(j + 1) * P], ident[:, :]),
                       sig=int(j == 3))
        oT = OA(lambda e, i: e.activation(actT[0], ps[:, TB, :].rearrange("p (j m) -> p j m", j=4), ACT.Copy), a)
        for c in range(2):
            for kk in range(KD):
                a = omm(ps[c * 64:c * 64 + 64, DB, :], actT[0][:, kk % 4, (kk // 4) * 64:(kk // 4) * 64 + 64],
                        wdn_o[:, kk, c * 512:(c + 1) * 512], kk == 0, kk == KD - 1, oT, oG,
                        sig=int(c == 1 and kk == KD - 1))
        oy = OA(lambda e, i: e.activation(yb[0], ps[:, DB, :], ACT.Copy), a)
        for t in range(2):
            for c in range(2):
                a = omm(ps[:, Y[t][c], :], GTo[c * 64:c * 64 + 64, t * P:(t + 1) * P], yb[0][c * 64:c * 64 + 64, :], True, True,
                        oy, oG, sig=int(t == 1 and c == 1))
        for t in range(2):
            for c in range(2):
                hs = h[:, t, c * 512:(c + 1) * 512]
                a_h = OV(lambda e, i, hs=hs, t=t, c=c: e.tensor_tensor(hs, hs, ps[:, Y[t][c], :], ALU.add), a)
        OD(lambda e, i: e.sem_inc(s_end, 1), (OV, OV.n), sig=0)

        def rounds(q, r, setup=lambda e: e.wait_ge(s_set, 1 + 2 * MORE)):
            def body(e):
                with e.If(most[q] >= CAP):
                    for s_, v in flat(loop_deps):
                        e.wait_ge(s_, v)
                    setup(e)
                    with e.Fori(0, MORE * NE) as i:
                        r.emit(e, i)

            q.raw(body)

        rounds(PE, OP)
        rounds(A, OA)
        rounds(V, OV, prepare)
        t_h = [V(lambda e: e.memset(sm[:, 298:299], 0.0))]
        t_pend = PE(lambda e: e.transpose(ps[0:1, TB, 0:P], m1, ident[:, :]), bank_free[TB])
        t_aend = A(lambda e: e.activation(sm[:, 299:300], m1, ACT.Copy))
        t_end = [t_h, t_pend, t_aend]
        bank_free[TB] = t_pend
        if stop == "moe":
            return run(finish(t_h))

        prow2 = ar(4096, 2, 256)
        pT = ar(4608, 2, T)
        gfin = ar(5120, 1024)
        Bb, PT3 = ar(0, 3072), ar(0, 3072)
        wbd = [ar(3072 + 512 * i, 4, P) for i in range(2)]
        S2 = ar(4096, 3072)
        q2, k2 = ar(7168, 4, T), ar(8192, 4, T)
        rg, ig = ar(7168, 4, T), ar(8192, 4, T)
        gmix, gffn = ar(9216, 1024), ar(10240, 1024)
        v2 = ar(11264, 2, 512)
        xr, gr, xc = (ar(12288 + 1024 * i, 4, T) for i in range(3))
        junk = ar(15360, 2, D)
        pp = ar(12288, 2, D)

        def gain_row(name, g, src, *waits):
            return dma(G, name, g, bc(src, [P, D]), *waits)

        t_moe = [gu_tok[NE - 1]]
        t_p = dma(G, "d_p", prow2, I["p"][0, 0].rearrange("(t p) d -> p t d", p=P), t_moe)
        t_gfin = gain_row("d_gfin", gfin, I["g_final"].rearrange("(a d) -> a d", a=1), t_moe)
        B0, B1 = halves(Bb)

        def skewed(off, n):
            return bass.AP(skew.tensor, off, [[511, P], [P * 512, 8], [1, n]])

        t_wz = G(lambda e: e.memset(ar(3072, 1024), 0.0), t_end)
        t_B = [dma(G, "d_B0", B0, skewed(255, P), t_end, t_skew),
               dma(G, "d_B1", B1, skewed(127, T), t_end, t_skew)]
        t_wbd = []
        for i, n in enumerate(("w_r_2", "w_i_2")):
            v = I[n][0].rearrange("(j s) c d -> s c j d", s=2)
            for s2 in range(2):
                t_wbd.append(dma(G, f"d_{n}{s2}", wbd[i][64 * s2:64 * s2 + 64, :, 64 * s2:64 * s2 + 64], v[s2], t_wz))
        t_gmix = gain_row("d_gmix", gmix, I["g_post_mix_2"], t_end)
        t_gffn = gain_row("d_gffn", gffn, I["g_post_ffn_2"], t_end)

        t_r = rstd([(h[:, t, :], junk[:, t, :], D) for t in range(2)], t_h, t_end)
        busy[:] = [t_pend, t_pend]
        parts, done, ahead = splitter(L_pg + L2_qk + L2_xg + L2_v + L2_o + L2_up + L2_dn)
        b = nb()
        for k in range(2):
            for t in range(2):
                last = tr(ps[:, b, k * T + t * P:k * T + (t + 1) * P], prow2[:, t, k * P:(k + 1) * P], t_p, bank_free[b],
                          t_end, sig=(k == 1 and t == 1))
        t_pT = bank_free[b] = act(pT, ps[:, b, :].rearrange("p (a b) -> p a b", a=2), ACT.Copy, last)
        bp, last2 = rows_product(pT, 2, [L_pp], 2, 1024, t_pT)
        t_uT = to_parts(h, *xin, 0, KD, lambda k: col("g_ple", k), t_h, t_pend)
        t_pp = []
        for t in range(2):
            for n in range(2):
                b = bp[t][n]
                bank_free[b] = act(pp[:, t, n * 512:(n + 1) * 512], ps[:, b, :], ACT.Copy, last2, t_end)
                t_pp.append(bank_free[b])
        ahead()
        prime(ACT.Sigmoid)
        bs, last = rows_parts(xin, range(KD), lambda k: (L_pg[k // 2], k % 2), 1024, lambda k: t_uT[k // 2], parts,
                              lambda n, tok: done(n, tok) if n != L_pg[3] else None)
        t_h, t_y, t_sq = [], [], []
        for t in range(2):
            for n in range(2):
                us = u[:, t, n * 512:(n + 1) * 512]
                a = bank_free[bs[t][n]] = act(us, ps[:, bs[t][n], :], ACT.Sigmoid, last, t_r, scale=rs[:, t:t + 1])
            a = vtt(u[:, t, :], u[:, t, :], pp[:, t, :], ALU.mult, a, t_pp)
            t_h.append(vtt(h[:, t, :], h[:, t, :], u[:, t, :], ALU.add, a, t_uT))
            t_y.append(vtt(u[:, t, :], h[:, t, :], gfin, ALU.mult, t_h[t], t_gfin))
        prime(ACT.Sqrt)
        for i, (src, ts) in enumerate(((h, t_h), (u, t_y))):
            for t in range(2):
                t_sq.append(act((junk, pp)[i][:, t, :], src[:, t, :], ACT.Square, ts[t], accum_out=ss[:, 2 * i + t:2 * i + t + 1]))
        r1, r2 = rs[:, 2:4], rs[:, 0:2]
        a = vts(r1, ss[:, 0:2], 1.0 / D, EPS, ALU.mult, ALU.add, t_sq[0:2])
        t_r = a = vrecip(r1, r1, act(r1, r1, ACT.Sqrt, a))
        a = vtt(r2, r1, r1, ALU.mult, a)
        a = vtt(r2, r2, ss[:, 2:4], ALU.mult, a, t_sq)
        a = vts(r2, r2, 1.0 / D, EPS, ALU.mult, ALU.add, a)
        a = vrecip(r2, r2, act(r2, r2, ACT.Sqrt, a))
        a = vtt(r2, r2, r1, ALU.mult, a)
        t_u = [vts(junk[:, t, :], u[:, t, :], rs[:, t:t + 1], None, ALU.mult, None, a, t_sq) for t in range(2)]
        t_uT = to_parts(junk, *xin, 0, KD, lambda k: col("g_pre_mix_2", k), t_u, last)
        t_h = [act(h[:, t, :], u[:, t, :], ACT.Copy, t_r, t_sq, scale=rs[:, 2 + t:3 + t]) for t in range(2)]
        done(L_pg[3], last)
        if stop == "ple":
            done_ = finish([t_h, t_B, t_wbd, t_gmix, t_gffn])
            return run(done_)

        t_ple = [t_r, t_uT, t_h]

        def two_columns(i, s, dsts):
            dst = dsts[i // 2][:, 2 * (i % 2):2 * (i % 2) + 2, :]
            b = nb()
            for m in range(2):
                tk = columns_parts(xin, s, m, ps[:, b, m * T:(m + 1) * T], [t_uT, bank_free[b]], parts)
            done(s, tk)
            bank_free[b] = act(dst, ps[:, b, :].rearrange("p (a b) -> p a b", a=2), ACT.Copy, tk, t_ple)
            return bank_free[b]

        tq = [two_columns(i, s, (q2, k2)) for i, s in enumerate(L2_qk)]
        b0, b1, t_scores = pair_scores(q2, k2, tq)
        S0, S1 = halves(S2)
        B0v = B0.rearrange("p (i s) k -> p s i k", s=2)
        B1v = B1.rearrange("p (i s) k -> p s i k", s=2)
        t_s = [[], []]
        for par in range(2):
            bank_free[b0[par]] = vstt(S0[:, 4 * par:4 * par + 4, :], ps[:, b0[par], :].rearrange("p (a b) -> p a b", a=4),
                                      SBS, B0v[:, par], ALU.mult, ALU.add, t_scores, t_B, t_ple)
            t_s[0].append(bank_free[b0[par]])
        for par in range(2):
            for i in range(2):
                b = b1[par][i]
                bank_free[b] = vstt(S1[:, 4 * par + 2 * i:4 * par + 2 * i + 2, :],
                                    ps[:, b, :].rearrange("p (a b) -> p a b", a=2), SBS,
                                    B1v[:, par, 2 * i:2 * i + 2], ALU.mult, ALU.add, t_scores, t_B, t_ple)
                t_s[1].append(bank_free[b])
        tx = [two_columns(i, s, (xr, gr)) for i, s in enumerate(L2_xg[:2])]
        t_xc = []
        for c in range(4):
            a = vts(xc[:, c, :], xr[:, c, :], col("w_conv_lru_2", 12 + c), col("b_conv_lru_2", c), ALU.mult, ALU.add, tx[c // 2],
                    t_ple)
            for d in (1, 2, 3):
                a = vstt(xc[:, c, d:], xr[:, c, 0:T - d], col("w_conv_lru_2", (3 - d) * 4 + c), xc[:, c, d:],
                         ALU.mult, ALU.add, a)
            t_xc.append(a)
        tx += [two_columns(2 + i, s, (xr, gr)) for i, s in enumerate(L2_xg[2:])]
        t_gr = []
        for g, (dst, bias) in enumerate(((rg, "b_r_2"), (ig, "b_i_2"))):
            for c in range(0, 4, 2):
                b = nb()
                for j in range(2):
                    tk = mm(ps[:, b, j * T:(j + 1) * T], wbd[g][:, c + j, :], xc[:, c + j, :], True, True, t_wbd, t_xc[c + j],
                            bank_free[b], sig=(j == 1))
                for j in range(2):
                    a = act(dst[:, c + j, :], ps[:, b, j * T:(j + 1) * T], ACT.Sigmoid, tk, t_scores, bias=col(bias, c + j))
                bank_free[b] = a
                t_gr.append(a)
        uf = u[:, :, :].rearrange("p t d -> p (t d)")
        av, tv_ = (uf[:, 1024 * i:1024 * i + 1024].rearrange("p (c t) -> p c t", c=4) for i in range(2))
        ta = [vts(rg[:, c, :], rg[:, c, :], lam0[:, c:c + 1], None, ALU.mult, None, t_gr, t_lam) for c in range(4)]
        t_a = act(av, rg, ACT.Exp, ta, t_uT, t_ple)
        t_e, t_r2 = softmax(S2, *t_s, True)
        bs, last = rows_parts(xin, range(KD), lambda k: (L2_v[k // 4], k % 4), 512, lambda k: t_uT, parts,
                              lambda n, tok: None)
        t_proj = last
        tk, _ = weigh_columns(S2, parity, PT3, lambda i: t_e[i], [t_s], [V, A])
        t_v = []
        for t in range(2):
            bank_free[bs[t][0]] = act(v2[:, t, :], ps[:, bs[t][0], :], ACT.Copy, last, t_ple)
            t_v.append(bank_free[bs[t][0]])
        t_r2 = softmax_sums(S2, t_r2, True)
        done(L2_v[0], t_proj)
        t_t = act(tv_, rg, ACT.Tanh, ta, t_uT, t_ple, scale=-1.0)
        done(L2_v[1], t_proj)
        t_ix = vtt(ig, ig, xc, ALU.mult, t_gr)
        a = vtt(rg, av, av, ALU.mult, t_t, t_a)
        a = vstt(tv_, rg, 1.0, tv_, ALU.add, ALU.mult, a)
        t_sq = act(tv_, tv_, ACT.Sqrt, a)
        bo, (_, last) = weigh_values(PT3, v2, tk, t_v)
        o2 = junk[:, 0, :].rearrange("p (t d) -> p t d", t=2)
        t_o = []
        for t in range(2):
            rv = rsum[:, 8 * t:8 * t + 8].rearrange("p (s i) -> p i s", s=2)
            o = o2[:, t, :].rearrange("p (i s d) -> p i s d", i=4, s=2)
            i = ps[:, bo[t], :].rearrange("p (i s d) -> p i s d", i=4, s=2)
            bank_free[bo[t]] = vtt(o, i, bc(rv.unsqueeze(3), [P, 4, 2, 64]), ALU.mult, last, t_r2, t_uT)
            t_o.append(bank_free[bo[t]])
        t_aT2 = []
        for k in range(0, 4, 2):
            b = nb()
            for j in range(2):
                for t in range(2):
                    a = tr(ps[:, b, j * T + t * P:j * T + (t + 1) * P], o2[:, t, (k + j) * P:(k + j + 1) * P], t_o,
                           bank_free[b], sig=(j == 1 and t == 1))
            i = ps[:, b, :].rearrange("p (a b) -> p a b", a=2)
            a = act(X[:, 0, k:k + 2, :], i, ACT.Copy, a, t_proj)
            bank_free[b] = vtt(X[:, 1, k:k + 2, :], i, X[:, 0, k:k + 2, :].bitcast(F32), ALU.subtract, a, t_proj)
            t_aT2.append(bank_free[b])
        t_gl = act(gr, gr, ACT.Gelu_apprx_tanh, tx)
        a = vtt(ig, ig, tv_, ALU.mult, t_ix, t_sq)
        t_lr = []
        for c in range(4):
            t = V(lambda e, c=c: e.tensor_tensor_scan(xr[:, c, :], av[:, c, :], ig[:, c, :], 0.0, ALU.mult, ALU.add),
                  a, t_a, t_xc)
            t = vtt(xr[:, c, :], xr[:, c, :], gr[:, c, :], ALU.mult, t, t_gl)
            x = act(X[:, 0, 4 + c, :], xr[:, c, :], ACT.Copy, t, t_proj)
            t_lr.append(vtt(X[:, 1, 4 + c, :], xr[:, c, :], X[:, 0, 4 + c, :].bitcast(F32), ALU.subtract, x, t_proj))
        prime(ACT.Sqrt)

        bs, last = rows_parts(xin, range(KD), lambda k: (L2_o[k // 2], k % 2), 1024,
                              lambda k: t_aT2[k // 2] if k < 4 else t_lr[k - 4], parts,
                              lambda n, tok: done(n, tok) if n != L2_o[3] else None)

        def add_normed(bs, gb, waits, t_gb, c0):
            toks = []
            for t in range(2):
                ts = [act(junk[:, t, n * 512:(n + 1) * 512], ps[:, bs[t][n], :], ACT.Square, waits,
                          accum_out=ss[:, 2 * t + n:2 * t + n + 1]) for n in range(2)]
                r = rs[:, c0 + t:c0 + t + 1]
                a = vtt(r, ss[:, 2 * t:2 * t + 1], ss[:, 2 * t + 1:2 * t + 2], ALU.add, ts)
                a = vts(r, r, 1.0 / D, EPS, ALU.mult, ALU.add, a)
                a = vrecip(r, r, act(r, r, ACT.Sqrt, a))
                for n in range(2):
                    c = slice(n * 512, (n + 1) * 512)
                    us = u[:, t, c]
                    g = bank_free[bs[t][n]] = vstt(us, ps[:, bs[t][n], :], r, gb[:, c], ALU.mult, ALU.mult, a, t_gb)
                    toks.append(vtt(h[:, t, c], h[:, t, c], us, ALU.add, g))
            return toks

        t_h = add_normed(bs, gmix, [last, t_lr], t_gmix, 0)
        if stop == "mix":
            done_ = finish([t_h, t_gffn])
            return run(done_)

        t_u = norm_rows(h, u, u, [(0, D)], c0=2, own=(t_h[0:2], t_h[2:4]))
        t_uT = to_parts(u, *xin, 0, KD, lambda k: col("g_pre_ffn_2", k), t_u, last)
        done(L2_o[3], last)
        fT = ar(0, 22, T)
        tmp = [ar(5632 + 256 * i, T) for i in range(8)]
        t_tmp = [None] * 8
        t_f = []

        def taps(c):
            return col("w_conv_ffn_2", c), col("w_conv_ffn_2", 44 + c), col("w_conv_ffn_2b", c), col("b_conv_ffn_2", c)

        def conv_tile(s, m, c, y, free):
            b = nb()
            tok = columns_parts(xin, s, m, ps[:, b, 0:T], [t_uT, bank_free[b]], parts)
            if m and s != L2_up[-1]:
                done(s, tok)
            elif m:
                for k in range(2):
                    inner_parts(k)
                done(s, tok)
            w0, w1, w2_, bb = taps(c)
            a = act(y, ps[:, b, 0:T], ACT.Identity, tok, free, scale=w2_, bias=bb)
            a = vstt(y[:, 1:], ps[:, b, 0:T - 1], w1, y[:, 1:], ALU.mult, ALU.add, a)
            bank_free[b] = vstt(y[:, 2:], ps[:, b, 0:T - 2], w0, y[:, 2:], ALU.mult, ALU.add, a)
            return bank_free[b]

        t_fp, t_free = [], [None] * 8

        def inner_parts(k):
            r = k % 8
            a = act(X[:, 0, r, :], fT[:, k, :], ACT.Copy, t_f[k], t_free[r] or PE.last())
            t_fp.append(vtt(X[:, 1, r, :], fT[:, k, :], X[:, 0, r, :].bitcast(F32), ALU.subtract, a))

        t_pv = [last, PE.last(), t_h, t_lr]
        prime(ACT.Gelu_apprx_tanh)
        for i in range(11):
            pend = []
            for half in range(2):
                for m in range(2):
                    c = 2 * i + m
                    y = (4 * (i % 2)) + 2 * half + m
                    pend.append(conv_tile(L2_up[2 * i + half], m, 22 * half + c, tmp[y], [t_tmp[y], t_pv]))
            for m in range(2):
                y = 4 * (i % 2) + m
                a = act(tmp[y + 2], tmp[y + 2], ACT.Gelu_apprx_tanh, pend[2 + m])
                t = vtt(fT[:, 2 * i + m, :], tmp[y], tmp[y + 2], ALU.mult, a, pend[m], t_pv)
                t_tmp[y] = t_tmp[y + 2] = t
                t_f.append(t)

        bs = [[nb(), nb()], [nb(), nb()]]
        for k in range(2, 6):
            inner_parts(k)
        for k in range(22):
            s = L2_dn[k // 2]
            hi, lo, ready, _ = parts[s]
            for t in range(2):
                for n in range(2):
                    c = slice(n * 512, (n + 1) * 512)
                    last = mm3(ps[:, bs[t][n], :], [y[:, k % 8, t * P:(t + 1) * P] for y in xin],
                               (hi[:, k % 2, c], lo[:, k % 2, c]), k == 0, k == 21,
                               [t_fp[k], ready, bank_free[bs[t][n]]], True, sig=(t == 1 and n == 1))
            t_free[k % 8] = last
            if k + 6 < 22:
                inner_parts(k + 6)
            if k % 2:
                done(s, last)
        prime(ACT.Sqrt)
        t_h = add_normed(bs, gffn, [last], t_gffn, 0)
        done_ = finish(t_h)
        run(done_)


_INS = ['x', 'p', 'positions', 'w_in', 'g_attn', 'g_cq', 'w_uq', 'g_ckv', 'w_ukv', 'g_out_mla', 'g_out_sb', 'w_o', 'g_moe',
        'w_router', 'b_router', 'w_gu', 'b_gu', 'w_dn', 'b_dn', 'g_ple', 'w_ple_gate', 'w_ple_proj', 'g_final',
        'g_pre_mix_2', 'w_in_2', 'rel_bias_2', 'w_conv_lru_2', 'b_conv_lru_2', 'w_r_2', 'b_r_2', 'w_i_2', 'b_i_2',
        'lam_2', 'w_out_2', 'g_post_mix_2', 'g_pre_ffn_2', 'w_up_2', 'w_conv_ffn_2', 'b_conv_ffn_2', 'w_down_2',
        'g_post_ffn_2']


def kernel(**inputs):
    import concourse.bacc as _bacc
    from concourse.bass_utils import run_bass_kernel_spmd as _run

    nc = _bacc.Bacc("TRN2", target_bir_lowering=False, num_devices=1)
    given = {name: np.ascontiguousarray(inputs[name]) for name in _INS}
    given["c_bucket"] = bucket_table()
    given["c_inv_freq"] = inv_freq_table()
    arrays, aps = {}, {}
    for name, a in given.items():
        arrays[f"in_{name}_dram"] = a
        aps[name] = nc.dram_tensor(f"in_{name}_dram", a.shape, mybir.dt.from_np(a.dtype), kind="ExternalInput").ap()
    out = nc.dram_tensor("out_0_dram", (1, T, D), F32, kind="ExternalOutput").ap()
    build_program(nc, aps, out)
    r = _run(nc, [arrays], core_ids=[0])
    return r.results[0]["out_0_dram"]
```
